# Optimizing a Trainium2 kernel written in Bass

```python
import functools
import math
import jax
import jax.numpy as jnp
from jax import lax
import numpy as np
import jax, jax.numpy as jnp

D_MODEL = 1024
BATCH = 1
SEQ = 256
DEPTH = 2

GRID_W = 64
CTX_LEN = 256
ROPE_THETA = 10000.0
NORM_EPS = 1e-6
NEG_INF = -1e30
BLOCK = 128
WINDOW = 128

A_HEADS = 8
A_KV_HEADS = 2
A_HEAD_DIM = 64
B_HEADS = 4
B_QK_DIM = 64
B_V_DIM = 2 * B_QK_DIM
A_Q_W = A_HEADS * A_HEAD_DIM
A_KV_W = A_KV_HEADS * A_HEAD_DIM
B_QK_W = B_HEADS * 2 * B_QK_DIM
B_V_W = B_HEADS * B_V_DIM
AB_Q_W = A_Q_W + B_QK_W
AB_IN_W = AB_Q_W + 2 * A_KV_W + B_QK_W + B_V_W
AB_OUT_W = A_Q_W + B_V_W

C_HEADS = 16
C_Q_LORA = 384
C_KV_LORA = 256
C_NOPE = 64
C_ROPE = 32
C_V = 64
C_IN_W = C_Q_LORA + C_KV_LORA + C_ROPE
C_OUT_W = C_HEADS * C_V

FFN_HIDDEN = ((8 * D_MODEL + 3 * 256 - 1) // (3 * 256)) * 256

N_EVEN = (DEPTH + 1) // 2
N_ODD = DEPTH // 2

F32 = jnp.float32


def rmsnorm(x, g):
    xf = x.astype(F32)
    y = xf * lax.rsqrt(jnp.mean(xf * xf, axis=-1, keepdims=True) + NORM_EPS)
    return (y * g.astype(F32)).astype(x.dtype)

def modulate(xn, shift, scale):
    return xn * (1.0 + scale) + shift

def joint_softmax(*logits):
    m = functools.reduce(jnp.maximum, [s.max(axis=-1, keepdims=True) for s in logits])
    e = [jnp.exp(s - m) for s in logits]
    inv = 1.0 / functools.reduce(jnp.add, [t.sum(axis=-1, keepdims=True) for t in e])
    return [t * inv for t in e]

def axial_rope_tables(rows, rot_dim):
    row = jnp.repeat(jnp.arange(rows, dtype=F32), GRID_W)
    col = jnp.tile(jnp.arange(GRID_W, dtype=F32), rows)
    axis_dim = rot_dim // 2
    inv_freq = ROPE_THETA ** (-jnp.arange(0, axis_dim, 2, dtype=F32) / axis_dim)
    ang = jnp.concatenate([row[:, None] * inv_freq, col[:, None] * inv_freq], axis=-1)
    return jnp.cos(ang), jnp.sin(ang)

def apply_axial_rope(x, tab):
    cos, sin = tab
    quarter = x.shape[-1] // 4
    xr, xc = jnp.split(x.astype(F32), 2, axis=-1)

    def rot(u, cs, sn):
        u1, u2 = jnp.split(u, 2, axis=-1)
        return jnp.concatenate([u1 * cs - u2 * sn, u2 * cs + u1 * sn], axis=-1)

    out = jnp.concatenate([
        rot(xr, cos[:, None, :quarter], sin[:, None, :quarter]),
        rot(xc, cos[:, None, quarter:], sin[:, None, quarter:])], axis=-1)
    return out.astype(x.dtype)

def to_blocks(t):
    b, n = t.shape[:2]
    return jnp.moveaxis(t.reshape(b, n // BLOCK, BLOCK, *t.shape[2:]), 1, 0)

def from_blocks(t):
    t = jnp.moveaxis(t, 0, 1)
    return t.reshape(t.shape[0], -1, *t.shape[3:])

def swiglu(h, w13, w2):
    gate, up = jnp.split(h @ w13, 2, axis=-1)
    return (jax.nn.silu(gate) * up) @ w2

def lambda_init(layer_idx):
    return 0.8 - 0.6 * math.exp(-0.3 * layer_idx)

def window_gqa_latent(q, k, v, k_ctx, v_ctx, sink):
    bsz, n, _, dh = q.shape
    nb = n // BLOCK
    g = A_HEADS // A_KV_HEADS
    scale = dh ** -0.5
    qb = q.reshape(bsz, nb, BLOCK, A_KV_HEADS, g, dh)

    def band(t):
        tp = jnp.pad(t, ((0, 0), (BLOCK, BLOCK), (0, 0), (0, 0)))
        tp = tp.reshape(bsz, nb + 2, BLOCK, A_KV_HEADS, dh)
        return jnp.concatenate([tp[:, :-2], tp[:, 1:-1], tp[:, 2:]], axis=2)

    kb, vb = band(k), band(v)
    s_loc = jnp.einsum('bnqhgd,bnkhd->bhgnqk', qb, kb).astype(F32) * scale
    s_ctx = jnp.einsum('bnqhgd,bchd->bhgnqc', qb, k_ctx).astype(F32) * scale
    qi = jnp.arange(BLOCK)[:, None]
    kj = jnp.arange(3 * BLOCK)[None, :]
    key_pos = (jnp.arange(nb)[:, None, None] - 1) * BLOCK + kj[None]
    valid = (jnp.abs(kj - BLOCK - qi) <= WINDOW)[None] & (key_pos >= 0) & (key_pos < n)
    s_loc = jnp.where(valid, s_loc, NEG_INF)
    s_sink = sink.astype(F32).reshape(1, A_KV_HEADS, g, 1, 1, 1)
    p_loc, p_ctx, _ = joint_softmax(s_loc, s_ctx, s_sink)
    o = (jnp.einsum('bhgnqk,bnkhd->bnqhgd', p_loc.astype(v.dtype), vb)
         + jnp.einsum('bhgnqc,bchd->bnqhgd', p_ctx.astype(v.dtype), v_ctx))
    return o.reshape(bsz, n, A_HEADS * dh)

def gqa_ctx(q, k, v, sink):
    bsz, t, _, dh = q.shape
    g = A_HEADS // A_KV_HEADS
    qg = q.reshape(bsz, t, A_KV_HEADS, g, dh)
    s = jnp.einsum('bqhgd,bkhd->bhgqk', qg, k).astype(F32) * dh ** -0.5
    p, _ = joint_softmax(s, sink.astype(F32).reshape(1, A_KV_HEADS, g, 1, 1))
    o = jnp.einsum('bhgqk,bkhd->bqhgd', p.astype(v.dtype), v)
    return o.reshape(bsz, t, A_HEADS * dh)

def diff_attend(q, kv_parts, lam):
    scale = q.shape[-1] ** -0.5
    logits = [jnp.einsum('bqhmd,bkhmd->bmhqk', q, k).astype(F32) * scale for k, _ in kv_parts]
    probs = joint_softmax(*logits)
    outs = [jnp.einsum('bhqk,bkhd->bqhd', (p[:, 0] - lam * p[:, 1]).astype(v.dtype), v)
            for p, (_, v) in zip(probs, kv_parts)]
    return functools.reduce(jnp.add, outs)

def diff_out(o, subln_g, lam_init):
    b, t = o.shape[:2]
    return (rmsnorm(o, subln_g) * (1.0 - lam_init)).reshape(b, t, -1)

def ab_queries(p_q):
    b, t = p_q.shape[:2]
    qa = p_q[..., :A_Q_W].reshape(b, t, A_HEADS, A_HEAD_DIM)
    qb = p_q[..., A_Q_W:].reshape(b, t, B_HEADS, 2, B_QK_DIM)
    return qa, qb

def ab_keys_values(p_kv):
    b, t = p_kv.shape[:2]
    o1 = A_KV_W
    o2 = 2 * A_KV_W
    o3 = o2 + B_QK_W
    ka = p_kv[..., :o1].reshape(b, t, A_KV_HEADS, A_HEAD_DIM)
    va = p_kv[..., o1:o2].reshape(b, t, A_KV_HEADS, A_HEAD_DIM)
    kb = p_kv[..., o2:o3].reshape(b, t, B_HEADS, 2, B_QK_DIM)
    vb = p_kv[..., o3:].reshape(b, t, B_HEADS, B_V_DIM)
    return ka, va, kb, vb

def rope_diff(t, tab):
    b, n = t.shape[:2]
    return apply_axial_rope(t.reshape(b, n, B_HEADS * 2, B_QK_DIM), tab).reshape(t.shape)

def mixer_ab(hx, hc, w_in, w_out, sink, lam_vec, subln_g, lam_init, tab, ctx_queries):
    p = hx @ w_in
    qa, qb = ab_queries(p[..., :AB_Q_W])
    ka, va, kb, vb = ab_keys_values(p[..., AB_Q_W:])
    qa, ka = apply_axial_rope(qa, tab), apply_axial_rope(ka, tab)
    qb, kb = rope_diff(qb, tab), rope_diff(kb, tab)
    if ctx_queries:
        pc = hc @ w_in
        cqa, cqb = ab_queries(pc[..., :AB_Q_W])
        cka, cva, ckb, cvb = ab_keys_values(pc[..., AB_Q_W:])
    else:
        cka, cva, ckb, cvb = ab_keys_values(hc @ w_in[:, AB_Q_W:])
    lv = lam_vec.astype(F32)
    lam = jnp.exp(jnp.sum(lv[0] * lv[1])) - jnp.exp(jnp.sum(lv[2] * lv[3])) + lam_init

    oa = window_gqa_latent(qa, ka, va, cka, cva, sink)
    ob = from_blocks(lax.map(lambda qblk: diff_attend(qblk, [(kb, vb), (ckb, cvb)], lam),
                             to_blocks(qb)))
    yx = jnp.concatenate([oa, diff_out(ob, subln_g, lam_init)], axis=-1) @ w_out
    if not ctx_queries:
        return yx, None
    oca = gqa_ctx(cqa, cka, cva, sink)
    ocb = diff_out(diff_attend(cqb, [(ckb, cvb)], lam), subln_g, lam_init)
    yc = jnp.concatenate([oca, ocb], axis=-1) @ w_out
    return yx, yc

def mla_queries(p_q, q_norm_g, wq_b):
    b, t = p_q.shape[:2]
    q = (rmsnorm(p_q, q_norm_g) @ wq_b).reshape(b, t, C_HEADS, C_NOPE + C_ROPE)
    return q[..., :C_NOPE], q[..., C_NOPE:]

def mla_keys_values(p_kv, kv_norm_g, wkv_b):
    b, t = p_kv.shape[:2]
    kv_lat, k_rope = p_kv[..., :C_KV_LORA], p_kv[..., C_KV_LORA:]
    kv = (rmsnorm(kv_lat, kv_norm_g) @ wkv_b).reshape(b, t, C_HEADS, C_NOPE + C_V)
    return kv[..., :C_NOPE], k_rope, kv[..., C_NOPE:]

def mla_attend(q_nope, q_rope, kv_parts):
    scale = (C_NOPE + C_ROPE) ** -0.5
    logits = [(jnp.einsum('bqhd,bkhd->bhqk', q_nope, kn)
               + jnp.einsum('bqhr,bkr->bhqk', q_rope, kr)).astype(F32) * scale
              for kn, kr, _ in kv_parts]
    probs = joint_softmax(*logits)
    outs = [jnp.einsum('bhqk,bkhd->bqhd', p.astype(v.dtype), v) for p, (_, _, v) in zip(probs, kv_parts)]
    return functools.reduce(jnp.add, outs)

def mixer_mla(hx, hc, w_in, q_norm_g, kv_norm_g, wq_b, wkv_b, w_out, tab, ctx_queries):
    bsz, n, _ = hx.shape
    p = hx @ w_in
    qn, qr = mla_queries(p[..., :C_Q_LORA], q_norm_g, wq_b)
    kn, kr, v = mla_keys_values(p[..., C_Q_LORA:], kv_norm_g, wkv_b)
    qr = apply_axial_rope(qr, tab)
    kr = apply_axial_rope(kr[:, :, None, :], tab)[:, :, 0, :]
    if ctx_queries:
        pc = hc @ w_in
        cqn, cqr = mla_queries(pc[..., :C_Q_LORA], q_norm_g, wq_b)
        ckn, ckr, cv = mla_keys_values(pc[..., C_Q_LORA:], kv_norm_g, wkv_b)
    else:
        ckn, ckr, cv = mla_keys_values(hc @ w_in[:, C_Q_LORA:], kv_norm_g, wkv_b)
    o = from_blocks(lax.map(lambda qs: mla_attend(qs[0], qs[1], [(kn, kr, v), (ckn, ckr, cv)]),
                            (to_blocks(qn), to_blocks(qr))))
    yx = o.reshape(bsz, n, C_OUT_W) @ w_out
    if not ctx_queries:
        return yx, None
    oc = mla_attend(cqn, cqr, [(ckn, ckr, cv)])
    yc = oc.reshape(bsz, hc.shape[1], C_OUT_W) @ w_out
    return yx, yc

def first_inputs(seed: int = 0) -> dict:
    key = jax.random.key(seed)
    ks = jax.random.split(key, 20)

    def nrm(k, shape, scale):
        return jax.random.normal(k, shape, F32) * scale

    d = D_MODEL
    return {
        'x': nrm(ks[0], (BATCH, SEQ, d), 1.0),
        'c': nrm(ks[1], (BATCH, d), 1.0),
        'ctx': nrm(ks[2], (BATCH, CTX_LEN, d), 1.0),
        'c_ctx': nrm(ks[3], (d,), 1.0),
        'ada_w': nrm(ks[4], (DEPTH, d, 6 * d), 0.5 * d ** -0.5),
        'ada_b': nrm(ks[5], (DEPTH, 6 * d), 0.01),
        'norm_g': 1.0 + nrm(ks[6], (DEPTH, 4, d), 0.05),
        'ffn_w13': nrm(ks[7], (DEPTH, d, 2 * FFN_HIDDEN), d ** -0.5),
        'ffn_w2': nrm(ks[8], (DEPTH, FFN_HIDDEN, d), FFN_HIDDEN ** -0.5),
        'ab_w_in': nrm(ks[9], (N_EVEN, d, AB_IN_W), d ** -0.5),
        'ab_w_out': nrm(ks[10], (N_EVEN, AB_OUT_W, d), AB_OUT_W ** -0.5),
        'ab_sink': nrm(ks[11], (N_EVEN, A_HEADS), 0.5),
        'diff_lambda': nrm(ks[12], (N_EVEN, 4, B_QK_DIM), 0.1),
        'diff_subln_g': 1.0 + nrm(ks[13], (N_EVEN, B_V_DIM), 0.05),
        'mla_w_in': nrm(ks[14], (N_ODD, d, C_IN_W), d ** -0.5),
        'mla_q_norm_g': 1.0 + nrm(ks[15], (N_ODD, C_Q_LORA), 0.05),
        'mla_kv_norm_g': 1.0 + nrm(ks[16], (N_ODD, C_KV_LORA), 0.05),
        'mla_wq_b': nrm(ks[17], (N_ODD, C_Q_LORA, C_HEADS * (C_NOPE + C_ROPE)), C_Q_LORA ** -0.5),
        'mla_wkv_b': nrm(ks[18], (N_ODD, C_KV_LORA, C_HEADS * (C_NOPE + C_V)), C_KV_LORA ** -0.5),
        'mla_w_out': nrm(ks[19], (N_ODD, C_OUT_W, d), C_OUT_W ** -0.5),
    }

def first_block(x, c, ctx, c_ctx, ada_w, ada_b, norm_g, ffn_w13, ffn_w2,
              ab_w_in, ab_w_out, ab_sink, diff_lambda, diff_subln_g,
              mla_w_in, mla_q_norm_g, mla_kv_norm_g, mla_wq_b, mla_wkv_b, mla_w_out):
    bsz, n, d = x.shape
    ROWS = n // GRID_W
    tab_ab = axial_rope_tables(ROWS, A_HEAD_DIM)
    tab_c = axial_rope_tables(ROWS, C_ROPE)
    sc_x = jax.nn.silu(c)
    sc_c = jax.nn.silu(c_ctx)
    for l in range(DEPTH):
        ctx_out = l < DEPTH - 1
        mx = (sc_x @ ada_w[l] + ada_b[l]).reshape(bsz, 6, 1, d)
        mc = (sc_c @ ada_w[l] + ada_b[l]).reshape(6, d)
        hx = modulate(rmsnorm(x, norm_g[l, 0]), mx[:, 0], mx[:, 1])
        hc = modulate(rmsnorm(ctx, norm_g[l, 0]), mc[0], mc[1])
        if l % 2 == 0:
            e = l // 2
            yx, yc = mixer_ab(hx, hc, ab_w_in[e], ab_w_out[e], ab_sink[e], diff_lambda[e],
                              diff_subln_g[e], lambda_init(l), tab_ab, ctx_out)
        else:
            o = l // 2
            yx, yc = mixer_mla(hx, hc, mla_w_in[o], mla_q_norm_g[o], mla_kv_norm_g[o],
                               mla_wq_b[o], mla_wkv_b[o], mla_w_out[o], tab_c, ctx_out)
        x = x + mx[:, 2] * rmsnorm(yx, norm_g[l, 1])
        hx = modulate(rmsnorm(x, norm_g[l, 2]), mx[:, 3], mx[:, 4])
        x = x + mx[:, 5] * rmsnorm(swiglu(hx, ffn_w13[l], ffn_w2[l]), norm_g[l, 3])
        if ctx_out:
            ctx = ctx + mc[2] * rmsnorm(yc, norm_g[l, 1])
            hc = modulate(rmsnorm(ctx, norm_g[l, 2]), mc[3], mc[4])
            ctx = ctx + mc[5] * rmsnorm(swiglu(hc, ffn_w13[l], ffn_w2[l]), norm_g[l, 3])
    return x


DEPTH_2 = 1

HGRN_HEADS = 4
HGRN_DK = 128
HGRN_DV = 128
HGRN_WIDTH = HGRN_HEADS * HGRN_DK
HGRN_CHUNK = 64
SGU_GROUPS = 4
SGU_CHUNK = 128
SGU_WIDTH = 512
SGU_GROUP_DIM = SGU_WIDTH // SGU_GROUPS
ROWS_PER_SGU_CHUNK = SGU_CHUNK // GRID_W
N_EXPERTS = 16
EXPERT_FF = 2048
CAPACITY_FACTOR = 2
N_MOD = 6
EPS = 1e-6
IN_COLS = 5 * HGRN_WIDTH + 2 * SGU_WIDTH + 2 * D_MODEL


def rmsnorm_2(x, w):
    xf = x.astype(jnp.float32)
    y = xf * lax.rsqrt(jnp.mean(xf * xf, axis=-1, keepdims=True) + EPS)
    return (y * w.astype(jnp.float32)).astype(x.dtype)

def adaln(cond, w, b):
    m = jax.nn.silu(cond) @ w + b
    m = m.reshape((-1, 1, N_MOD * D_MODEL))
    return jnp.split(m, N_MOD, axis=-1)

def modulate_2(h, shift, scale):
    return h * (1 + scale) + shift

def split_in(p):
    sizes = (HGRN_WIDTH,) * 5 + (SGU_WIDTH,) * 2 + (D_MODEL,) * 2
    idx = []
    acc = 0
    for s in sizes[:-1]:
        acc += s
        idx.append(acc)
    return jnp.split(p, idx, axis=-1)

def to_heads(a):
    return a.reshape(a.shape[0], a.shape[1], HGRN_HEADS, HGRN_DK)

def hgrn_forget(z, lb):
    f = lb + (1 - lb) * jax.nn.sigmoid(z.astype(jnp.float32))
    return jnp.log(f), 1 - f

def hgrn_chunk_scan(q, k, logf, v, s0):
    B_, T, H, DK = q.shape
    DV = v.shape[-1]
    nc = T // HGRN_CHUNK

    def to_chunks(a):
        return a.astype(jnp.float32).reshape(B_, nc, HGRN_CHUNK, H, a.shape[-1]).transpose(1, 0, 3, 2, 4)

    qc, kc, fc, vc = to_chunks(q), to_chunks(k), to_chunks(logf), to_chunks(v)
    mask = jnp.tril(jnp.ones((HGRN_CHUNK, HGRN_CHUNK), dtype=bool))[None, None, :, :, None]

    def step(S, inp):
        qb, kb, fb, vb = inp
        b = jnp.cumsum(fb, axis=2)
        diff = b[:, :, :, None, :] - b[:, :, None, :, :]
        decay = jnp.exp(jnp.where(mask, diff, -jnp.inf))
        scores = jnp.einsum('bhik,bhijk->bhij', qb, decay * kb[:, :, None, :, :])
        o = jnp.einsum('bhij,bhjv->bhiv', scores, vb) + jnp.einsum('bhik,bhkv->bhiv', qb * jnp.exp(b), S)
        b_last = b[:, :, -1:, :]
        S_new = jnp.exp(b_last[:, :, 0, :])[..., None] * S + jnp.einsum('bhjk,bhjv->bhkv', kb * jnp.exp(b_last - b), vb)
        return S_new, o

    s_fin, o = lax.scan(step, s0.astype(jnp.float32), (qc, kc, fc, vc))
    o = o.transpose(1, 0, 3, 2, 4).reshape(B_, T, H, DV)
    return o, s_fin

def hgrn_final_state(k, logf, v):
    b = jnp.cumsum(logf.astype(jnp.float32), axis=1)
    w = k.astype(jnp.float32) * jnp.exp(b[:, -1:] - b)
    return jnp.einsum('bthk,bthv->bhkv', w, v.astype(jnp.float32))

def sgu(u, v, norm_w, w_s, b_s, n_chunks):
    B_, T, _ = u.shape
    u = jax.nn.gelu(u).reshape(B_, n_chunks, SGU_CHUNK, SGU_GROUPS, SGU_GROUP_DIM)
    v = jax.nn.gelu(v).reshape(B_, T, SGU_GROUPS, SGU_GROUP_DIM)
    v = rmsnorm_2(v, norm_w.reshape(SGU_GROUPS, SGU_GROUP_DIM))
    v = v.reshape(B_, n_chunks, SGU_CHUNK, SGU_GROUPS, SGU_GROUP_DIM)
    mixed = jnp.einsum('gts,bnsgc->bntgc', w_s, v) + b_s.T[:, :, None]
    return (u * mixed).reshape(B_, T, SGU_WIDTH)

def token_mixer(parts, lb_f, lb_b, hgrn_norm_w, sgu_norm_w, sgu_w, sgu_b,
                w_branch_a, w_branch_b, w_out, s0_f, s0_b, n_sgu_chunks):
    q_p, ff_p, fb_p, v_p, g_p, u_p, sv_p, ga_p, gb_p = parts
    q = jax.nn.silu(to_heads(q_p))
    v = to_heads(v_p)
    logf_f, k_f = hgrn_forget(to_heads(ff_p), lb_f)
    logf_b, k_b = hgrn_forget(to_heads(fb_p), lb_b)
    o_f, s_f = hgrn_chunk_scan(q, k_f, logf_f, v, s0_f)
    o_b, s_b = hgrn_chunk_scan(q[:, ::-1], k_b[:, ::-1], logf_b[:, ::-1], v[:, ::-1], s0_b)
    o = o_f + o_b[:, ::-1]
    o = rmsnorm_2(o, hgrn_norm_w.reshape(HGRN_HEADS, HGRN_DV)).astype(g_p.dtype)
    o = o.reshape(o.shape[0], o.shape[1], HGRN_WIDTH) * jax.nn.silu(g_p)
    y_a = o @ w_branch_a
    y_b = sgu(u_p, sv_p, sgu_norm_w, sgu_w, sgu_b, n_sgu_chunks) @ w_branch_b
    merged = jax.nn.sigmoid(ga_p) * y_a + jax.nn.sigmoid(gb_p) * y_b
    return merged @ w_out, s_f, s_b

def moe_expert_choice(h, router_w, w_gate, w_up, w_down):
    B_, T, _ = h.shape
    cap = CAPACITY_FACTOR * T // N_EXPERTS
    aff = jax.nn.softmax((h @ router_w).astype(jnp.float32), axis=-1)
    gate, idx = lax.top_k(jnp.swapaxes(aff, 1, 2), cap)
    bidx = jnp.arange(B_)[:, None, None]
    xs = h[bidx, idx]
    hid = jax.nn.silu(jnp.einsum('becd,edf->becf', xs, w_gate)) * jnp.einsum('becd,edf->becf', xs, w_up)
    ye = jnp.einsum('becf,efd->becd', hid, w_down) * gate[..., None].astype(h.dtype)
    return jnp.zeros_like(h).at[bidx, idx].add(ye)

def second_inputs(seed: int = 0) -> dict:
    key = jax.random.key(seed)
    ks = jax.random.split(key, 24)
    f32 = jnp.float32
    nrm = lambda k, shape, s: jax.random.normal(k, shape, f32) * s
    return {
        'x': nrm(ks[0], (BATCH, SEQ, D_MODEL), 1.0),
        'c': nrm(ks[1], (BATCH, D_MODEL), 1.0),
        'ctx': nrm(ks[2], (BATCH, CTX_LEN, D_MODEL), 1.0),
        'c_ctx': nrm(ks[3], (D_MODEL,), 1.0),
        'ada_w': nrm(ks[4], (DEPTH_2, D_MODEL, N_MOD * D_MODEL), 0.02),
        'ada_b': nrm(ks[5], (DEPTH_2, N_MOD * D_MODEL), 0.02),
        'norm_mix_w': 1 + nrm(ks[6], (DEPTH_2, D_MODEL), 0.05),
        'norm_ffn_w': 1 + nrm(ks[7], (DEPTH_2, D_MODEL), 0.05),
        'w_in': nrm(ks[8], (DEPTH_2, D_MODEL, IN_COLS), D_MODEL ** -0.5),
        'hgrn_lb_logits': nrm(ks[9], (2, DEPTH_2 + 1, HGRN_WIDTH), 0.5),
        'hgrn_norm_w': 1 + nrm(ks[10], (DEPTH_2, HGRN_WIDTH), 0.05),
        'sgu_norm_w': 1 + nrm(ks[11], (DEPTH_2, SGU_WIDTH), 0.05),
        'sgu_w': nrm(ks[12], (DEPTH_2, SGU_GROUPS, SGU_CHUNK, SGU_CHUNK), SGU_CHUNK ** -0.5),
        'sgu_b': 1 + nrm(ks[13], (DEPTH_2, SGU_GROUPS, SGU_CHUNK), 0.05),
        'w_branch_a': nrm(ks[14], (DEPTH_2, HGRN_WIDTH, D_MODEL), HGRN_WIDTH ** -0.5),
        'w_branch_b': nrm(ks[15], (DEPTH_2, SGU_WIDTH, D_MODEL), SGU_WIDTH ** -0.5),
        'w_out': nrm(ks[16], (DEPTH_2, D_MODEL, D_MODEL), D_MODEL ** -0.5),
        'router_w': nrm(ks[17], (DEPTH_2, D_MODEL, N_EXPERTS), D_MODEL ** -0.5),
        'expert_w_gate': nrm(ks[18], (DEPTH_2, N_EXPERTS, D_MODEL, EXPERT_FF), D_MODEL ** -0.5),
        'expert_w_up': nrm(ks[19], (DEPTH_2, N_EXPERTS, D_MODEL, EXPERT_FF), D_MODEL ** -0.5),
        'expert_w_down': nrm(ks[20], (DEPTH_2, N_EXPERTS, EXPERT_FF, D_MODEL), EXPERT_FF ** -0.5),
        'final_norm_w': 1 + nrm(ks[21], (D_MODEL,), 0.05),
    }

def second_block(x, c, ctx, c_ctx, ada_w, ada_b, norm_mix_w, norm_ffn_w, w_in, hgrn_lb_logits,
              hgrn_norm_w, sgu_norm_w, sgu_w, sgu_b, w_branch_a, w_branch_b, w_out, router_w,
              expert_w_gate, expert_w_up, expert_w_down, final_norm_w):
    B_, N, _ = x.shape
    ROWS = N // GRID_W
    n_sgu_lat = ROWS // ROWS_PER_SGU_CHUNK
    n_sgu_ctx = ctx.shape[1] // SGU_CHUNK
    lb_all = jnp.cumsum(jax.nn.softmax(hgrn_lb_logits.astype(jnp.float32), axis=1), axis=1)
    for l in range(DEPTH_2):
        last = l == DEPTH_2 - 1
        lb_f = lb_all[0, l].reshape(HGRN_HEADS, HGRN_DK)
        lb_b = lb_all[1, l].reshape(HGRN_HEADS, HGRN_DK)
        sh_m, sc_m, g_m, sh_f, sc_f, g_f = adaln(c, ada_w[l], ada_b[l])
        csh_m, csc_m, cg_m, csh_f, csc_f, cg_f = adaln(c_ctx, ada_w[l], ada_b[l])

        h_ctx = modulate_2(rmsnorm_2(ctx, norm_mix_w[l]), csh_m, csc_m)
        pc = split_in(h_ctx @ w_in[l])
        if last:
            v_c = to_heads(pc[3])
            logf_f, k_f = hgrn_forget(to_heads(pc[1]), lb_f)
            logf_b, k_b = hgrn_forget(to_heads(pc[2]), lb_b)
            s_f = hgrn_final_state(k_f, logf_f, v_c)
            s_b = hgrn_final_state(k_b[:, ::-1], logf_b[:, ::-1], v_c[:, ::-1])
        else:
            zeros = jnp.zeros((ctx.shape[0], HGRN_HEADS, HGRN_DK, HGRN_DV), jnp.float32)
            y_c, s_f, s_b = token_mixer(pc, lb_f, lb_b, hgrn_norm_w[l], sgu_norm_w[l], sgu_w[l], sgu_b[l],
                                        w_branch_a[l], w_branch_b[l], w_out[l], zeros, zeros, n_sgu_ctx)
            ctx = ctx + cg_m * y_c
            h2c = modulate_2(rmsnorm_2(ctx, norm_ffn_w[l]), csh_f, csc_f)
            ctx = ctx + cg_f * moe_expert_choice(h2c, router_w[l], expert_w_gate[l], expert_w_up[l], expert_w_down[l])

        h = modulate_2(rmsnorm_2(x, norm_mix_w[l]), sh_m, sc_m)
        pl = split_in(h @ w_in[l])
        y, _, _ = token_mixer(pl, lb_f, lb_b, hgrn_norm_w[l], sgu_norm_w[l], sgu_w[l], sgu_b[l],
                              w_branch_a[l], w_branch_b[l], w_out[l], s_f, s_b, n_sgu_lat)
        x = x + g_m * y
        h2 = modulate_2(rmsnorm_2(x, norm_ffn_w[l]), sh_f, sc_f)
        x = x + g_f * moe_expert_choice(h2, router_w[l], expert_w_gate[l], expert_w_up[l], expert_w_down[l])
    return rmsnorm_2(x, final_norm_w)


def setup_inputs(seed=0):
    out = dict(first_inputs(seed))
    for name, value in second_inputs(seed + 1).items():
        if name != "x":
            out[name + "_2"] = value
    return out


def reference(
    x, c, ctx, c_ctx, ada_w, ada_b, norm_g, ffn_w13, ffn_w2, ab_w_in, ab_w_out, ab_sink,
    diff_lambda, diff_subln_g, mla_w_in, mla_q_norm_g, mla_kv_norm_g, mla_wq_b, mla_wkv_b,
    mla_w_out, c_2, ctx_2, c_ctx_2, ada_w_2, ada_b_2, norm_mix_w_2, norm_ffn_w_2, w_in_2,
    hgrn_lb_logits_2, hgrn_norm_w_2, sgu_norm_w_2, sgu_w_2, sgu_b_2, w_branch_a_2, w_branch_b_2,
    w_out_2, router_w_2, expert_w_gate_2, expert_w_up_2, expert_w_down_2, final_norm_w_2,
):
    x = first_block(
        x, c, ctx, c_ctx, ada_w, ada_b, norm_g, ffn_w13, ffn_w2, ab_w_in, ab_w_out, ab_sink,
        diff_lambda, diff_subln_g, mla_w_in, mla_q_norm_g, mla_kv_norm_g, mla_wq_b, mla_wkv_b,
        mla_w_out,
    )
    return second_block(
        x, c_2, ctx_2, c_ctx_2, ada_w_2, ada_b_2, norm_mix_w_2, norm_ffn_w_2, w_in_2,
        hgrn_lb_logits_2, hgrn_norm_w_2, sgu_norm_w_2, sgu_w_2, sgu_b_2, w_branch_a_2,
        w_branch_b_2, w_out_2, router_w_2, expert_w_gate_2, expert_w_up_2, expert_w_down_2,
        final_norm_w_2,
    )


_drawn_inputs = setup_inputs


def setup_inputs(seed=0):
    import zlib

    import numpy as np

    out = dict(_drawn_inputs(seed))
    spreads = {}
    factors = {'ab_sink': 8.0,
     'diff_lambda': 2.82,
     'diff_subln_g': 2.972,
     'mla_q_norm_g': 8.0,
     'mla_kv_norm_g': 3.647,
     'ctx_2': 6.524,
     'c_ctx_2': 8.0,
     'ada_b_2': 2.875,
     'norm_mix_w_2': 3.489,
     'norm_ffn_w_2': 3.742,
     'hgrn_lb_logits_2': 8.0,
     'hgrn_norm_w_2': 8.0,
     'sgu_norm_w_2': 6.056,
     'sgu_b_2': 6.521}
    for name, (base, spread) in spreads.items():
        noise = np.random.default_rng([zlib.crc32(name.encode()), seed]).standard_normal(out[name].shape)
        drawn = base * np.exp(spread * noise) if base else spread * noise
        out[name] = jnp.asarray(drawn.astype(out[name].dtype))
    for name, factor in factors.items():
        out[name] = (out[name] * factor).astype(out[name].dtype)
    return out
```

```python
import math
from contextlib import ExitStack

import concourse.bass as bass
import numpy as np
from concourse import mybir

ALU = mybir.AluOpType
ACT = mybir.ActivationFunctionType
F32 = mybir.dt.float32
U8 = mybir.dt.uint8
AX_X = mybir.AxisListType.X

P = 128
D = 1024
KD = D // P
TX = 256
T2 = 2 * TX
GRID_W = 64
THETA = 10000.0
EPS = 1e-6
NEG = -1e30
WINDOW = 128

AH, AKV, DH = 8, 2, 64
BH, BV = 4, 128
FFN = ((8 * D + 3 * 256 - 1) // (3 * 256)) * 256
KF = FFN // P
CH, QL, KVL, NOPE, ROPE, CV = 16, 384, 256, 64, 32, 64
CQK = NOPE + ROPE
LAM_INIT = 0.8 - 0.6 * math.exp(0.0)

HH = 4
HW_ = HH * P
SG = 4
NE, EF, CAP = 16, 2048, 32
LEVELS = [64, 32, 16, 8, 4, 2, 1]

SLOTS = 6
SLOT = 4096
BANKS = 8
TURN = 7
SMALL = 16 * 2
JPE = 12

FT = {}
_at = 0
for _n, _w in (("ident", 128), ("ones", 128), ("perm_ab", 128), ("perm_c", 128), ("cos_ab", 256), ("sin_ab", 256),
               ("cos_c", 256), ("sin_c", 256), ("window", 512), ("slot", 32), ("eps", 1),
               ("before", 512)):
    FT[_n] = (_at, _w)
    _at += _w
TAB_W = _at
FT_W = FT["before"][0]
VT = {}
_at = 0
for _n, _w in (("ada_b0", 48), ("ada_b1", 48), ("c", 8), ("c_ctx", 8), ("c_2", 8), ("c_ctx_2", 8),
               ("ada_b2", 48), ("norm_g", 64), ("norm_mix", 8), ("norm_ffn", 8),
               ("final", 8), ("subln", 1), ("q_norm", 3), ("kv_norm", 2), ("lb", 16), ("hgrn_norm", 4)):
    VT[_n] = _at
    _at += _w
VT_W = _at

def tables():
    f = np.zeros((P, TAB_W), np.float32)

    def put(name, a):
        o, w = FT[name]
        f[:a.shape[0], o:o + a.shape[1]] = a

    put("ident", np.eye(P, dtype=np.float32))
    put("ones", np.ones((P, P), np.float32))

    def rope(dim):
        t = np.arange(TX)
        axis = dim // 2
        inv = (np.float32(THETA) ** (-np.arange(0, axis, 2, dtype=np.float32) / np.float32(axis))).astype(np.float32)
        row = (t // GRID_W).astype(np.float32)[:, None] * inv
        col = (t % GRID_W).astype(np.float32)[:, None] * inv
        q = dim // 4
        ang = np.concatenate([row, row, col, col], 1).T
        perm = np.zeros((dim, dim), np.float32)
        for half in (0, 2 * q):
            for i in range(q):
                perm[half + q + i, half + i] = -1.0
                perm[half + i, half + q + i] = 1.0
        return np.cos(ang).astype(np.float32), np.sin(ang).astype(np.float32), perm

    c, s, p = rope(DH)
    put("cos_ab", np.concatenate([c, c]))
    put("sin_ab", np.concatenate([s, s]))
    put("perm_ab", np.kron(np.eye(2, dtype=np.float32), p))
    c, s, p = rope(ROPE)
    put("cos_c", np.concatenate([np.ones((NOPE, TX), np.float32), c]))
    put("sin_c", np.concatenate([np.zeros((NOPE, TX), np.float32), s]))
    pc = np.zeros((CQK, CQK), np.float32)
    pc[NOPE:, NOPE:] = p
    put("perm_c", pc)
    q = np.arange(TX)[:, None]
    k = np.arange(TX)[None, :]
    win = np.where(abs(q - k) <= WINDOW, 0.0, NEG).astype(np.float32)
    put("window", np.concatenate([win[:P], win[P:]], 1))
    bef = (k < q).astype(np.float32)
    put("before", np.concatenate([bef[:P], bef[P:]], 1))
    put("slot", np.tile(np.arange(CAP, dtype=np.float32), (P, 1)))
    put("eps", np.full((P, 1), EPS, np.float32))
    j = np.arange(P)[:, None]
    i = np.arange(P)[None, :]
    m = []
    for s in LEVELS:
        same = (j // (2 * s)) == (i // (2 * s))
        m.append(same & ((j // s) % 2 == 0) & ((i // s) % 2 == 1))
        m.append(same & ((j // s) % 2 == 1) & ((i // s) % 2 == 0))
    m.append(i == j)
    return f, np.concatenate(m, 1).astype(np.float32)

MASK_W = (2 * len(LEVELS) + 1) * P

def vector_rows(a):
    flat = np.zeros((3 * P, P), np.float32)
    for name, v in (("ada_b0", a["ada_b"][0]), ("ada_b1", a["ada_b"][1]), ("c", a["c"]), ("c_ctx", a["c_ctx"]),
                    ("c_2", a["c_2"]), ("c_ctx_2", a["c_ctx_2"]), ("ada_b2", a["ada_b_2"]), ("norm_g", a["norm_g"]),
                    ("norm_mix", a["norm_mix_w_2"]), ("norm_ffn", a["norm_ffn_w_2"]), ("final", a["final_norm_w_2"]),
                    ("subln", a["diff_subln_g"]), ("q_norm", a["mla_q_norm_g"]), ("kv_norm", a["mla_kv_norm_g"]),
                    ("lb", a["hgrn_lb_logits_2"]), ("hgrn_norm", a["hgrn_norm_w_2"])):
        v = np.asarray(v).reshape(-1, P)
        flat[VT[name]:VT[name] + len(v)] = v
    return np.ascontiguousarray(flat.reshape(3, P, P).transpose(1, 0, 2))


class Signal:

    def __init__(self, sem):
        self.sem, self.planned = sem, 0

    def plan(self, n):
        base = self.planned
        self.planned += n
        return base

def build(nc, A, tab_f, tab_m, vrows, out, last=99):
    es = ExitStack()
    with es:
        def sb(name, shape, dt=F32):
            return es.enter_context(nc.sbuf_tensor(name, shape, dt))

        def sem(name):
            return es.enter_context(nc.semaphore(name))

        ring = sb("ring", [P, SLOTS, SLOT])
        X = sb("X", [P, KD, T2])
        H = sb("H", [P, KD, T2])
        AR = sb("AR", [P, 15360])
        FTAB = sb("FTAB", [P, FT_W])
        MASK = sb("MASK", [P, MASK_W], U8)
        VEC = sb("VEC", [P, 3 * P])
        MOD = sb("MOD", [P, 3, 48, 2])
        AMP = sb("AMP", [P, 3, 2, KD, 2])
        GATE = sb("GATE", [P, 2, 2, KD, 2])
        RS = sb("RS", [P, T2])
        SC = sb("SC", [P, KD, 2, 32])
        ST = sb("ST", [P, 2, 8])
        SINK = sb("SINK", [P, AH])
        LAM = sb("LAM", [P, 8])
        LB = sb("LB", [P, 6, 8])
        SGS = sb("SGS", [P, 16])
        RTR = sb("RTR", [P, 72])
        ps = es.enter_context(nc.psum_tensor("ps", [P, BANKS, 512], F32))

        def ft(name, n=None, p=P):
            o, w = FT[name]
            return FTAB[0:p, o:o + (n or w)]

        def vec(name, i=0, n=1):
            return VEC[:, VT[name] + i:VT[name] + i + n]

        ident, ones = ft("ident"), ft("ones")

        def ar(off, *dims):
            n = int(np.prod(dims))
            a = AR[:, off:off + n]
            if len(dims) == 1:
                return a
            names = "abc"[:len(dims)]
            return a.rearrange(f"p ({' '.join(names)}) -> p {' '.join(names)}", **dict(zip(names, dims)))

        small_loaded = sem("small_loaded")
        slot_loaded = [sem(f"slot_loaded{i}") for i in range(SLOTS)]
        weights_used = sem("weights_used")
        bank_full = [sem(f"bank_full{i}") for i in range(BANKS)]
        bank_free = [sem(f"bank_free{i}") for i in range(BANKS)]
        out_written = sem("out_written")
        dve_step, act_step = sem("dve_step"), sem("act_step")
        cond_ready = sem("cond_ready")
        fg_ready = sem("fg_ready")
        sums_ready = sem("sums_ready")
        left_ready = sem("left_ready")
        kw_ready = sem("kw_ready")
        diff_ready = sem("diff_ready")
        decay_ready = sem("decay_ready")
        qk_ready = sem("qk_ready")
        svsum_ready = sem("svsum_ready")
        svr_ready = sem("svr_ready")
        sv_ready = sem("sv_ready")
        y_ready = sem("y_ready")
        rmax_ready = sem("rmax_ready")
        aff_ready = sem("aff_ready")
        pick_ready = sem("pick_ready")
        ctx_loaded = sem("ctx_loaded")
        late_loaded = sem("late_loaded")
        xse_ready = sem("xse_ready")
        side_loaded = sem("side_loaded")
        gates_ready = sem("gates_ready")
        x_loaded = sem("x_loaded")
        silu_done = sem("silu_done")
        hid_done = sem("hid_done")
        turned = sem("turned")
        hidt_ready = sem("hidt_ready")
        ye_ready = sem("ye_ready")
        fin_ready = sem("fin_ready")
        expert_loaded = [sem(f"expert_loaded{i}") for i in range(SLOTS)]
        squares_ready = Signal(sem("squares_ready"))
        rstd_ready = Signal(sem("rstd_ready"))
        scaled_ready = Signal(sem("scaled_ready"))
        h_ready = Signal(sem("h_ready"))
        x_ready = Signal(sem("x_ready"))
        roped = Signal(sem("roped"))
        stat_ready = Signal(sem("stat_ready"))
        probs_ready = Signal(sem("probs_ready"))
        o_ready = Signal(sem("o_ready"))
        lat_ready = Signal(sem("lat_ready"))
        logf_ready = Signal(sem("logf_ready"))

        jobs, job_at = [], {}

        def job(label, *dmas):
            job_at[label] = len(jobs)
            jobs.append(dmas)

        def rows(w, r0, r1, c0, c1):
            k, n = (r1 - r0) // P, c1 - c0
            return (lambda s: ring[:, s, 0:k * n].rearrange("p (k n) -> p k n", k=k),
                    w[r0:r1, c0:c1].rearrange("(k p) n -> p k n", p=P))

        def ada_jobs(l):
            w = A["ada_w_2"][0] if l == 2 else A["ada_w"][l]
            for i in range(12):
                g, k = i // 4, 2 * (i % 4)
                job(("ada", l, i), rows(w, k * P, (k + 2) * P, g * 2048, (g + 1) * 2048))

        def ffn_jobs(l):
            w13, w2 = A["ffn_w13"][l], A["ffn_w2"][l]
            for i in range(KF // 2):
                def dst(half):
                    return lambda s: ring[:, s, :].rearrange("p (k g n) -> p k g n", k=KD, g=2)[:, :, half, :]
                job(("w13", l, i), *((dst(h), w13[:, h * FFN + i * 256:h * FFN + (i + 1) * 256]
                                      .rearrange("(k p) n -> p k n", p=P)) for h in range(2)))
            for n in range(KD):
                job(("w2", l, n), rows(w2, 0, FFN, n * P, (n + 1) * P))

        AB_COLS = [(0, 512), (512, 1024), (1024, 1280), (1280, 1792), (1792, 2304)]
        ada_jobs(0)
        for i, (a, b) in enumerate(AB_COLS):
            job(("ab_in", i), rows(A["ab_w_in"][0], 0, D, a, b))
        ada_jobs(1)
        ada_jobs(2)
        for i in range(2):
            job(("ab_out", i), rows(A["ab_w_out"][0], 0, D, i * 512, (i + 1) * 512))
        ffn_jobs(0)
        mw = A["mla_w_in"][0]
        job("mla_q", rows(mw, 0, D, 0, QL))
        job("mla_kv", rows(mw, 0, D, QL, QL + KVL + ROPE))
        for i in range(2):
            job(("wq_b", i), rows(A["mla_wq_b"][0], 0, QL, i * 768, (i + 1) * 768))
        job("wkv_b", rows(A["mla_wkv_b"][0], 0, KVL, 0, 2048))
        for i in range(2):
            job(("mla_out", i), rows(A["mla_w_out"][0], 0, D, i * 512, (i + 1) * 512))
        ffn_jobs(1)
        for i in range(11):
            c = [512, 1024, 1536, 0, 2048, 2560, 3072, 3584, 4096, 4608, 5120][i]
            job(("in2", i), rows(A["w_in_2"][0], 0, D, c, c + 512))
        job("branch_a", rows(A["w_branch_a_2"][0], 0, 512, 0, D))
        job("branch_b", rows(A["w_branch_b_2"][0], 0, 512, 0, D))
        for i in range(2):
            job(("out2", i), rows(A["w_out_2"][0], 0, D, i * 512, (i + 1) * 512))
        NJ = len(jobs)
        loads = [0] * SLOTS
        loaded_at = []
        for j, dmas in enumerate(jobs):
            loads[j % SLOTS] += len(dmas)
            loaded_at.append(16 * loads[j % SLOTS])

        place, takes = {}, [0] * BANKS
        owed = [0]

        def take(pe, key, fixed=False):
            b = BANKS - 1 if fixed else sum(n for n in takes[:TURN]) % TURN
            use = takes[b]
            takes[b] += 1
            place[key] = (b, use + 1)
            if use:
                pe.wait_ge(bank_free[b], use)
            return b

        def mm(out_, lhsT, rhs, start, stop, full=None):
            m = nc.tensor.matmul(out_, lhsT=lhsT, rhs=rhs, start=start, stop=stop)
            if full is not None:
                m.then_inc(bank_full[full], 1)
            elif owed[0]:
                m.then_inc(weights_used, 1)
                owed[0] -= 1
            return m

        def weights(pe, label):
            j = job_at[label]
            pe.wait_ge(slot_loaded[j % SLOTS], loaded_at[j])
            return ring[:, j % SLOTS, :]

        def used():
            owed[0] += 1
            assert owed[0] == 1

        def full_of(eng, key):
            b, use = place[key]
            eng.wait_ge(bank_full[b], use)
            return b

        def freed(eng, key):
            b, use = place[key]
            eng.wait_ge(bank_free[b], use)

        def pe_dense(pe, key, w, col, H_, T, K=KD, M=P, pre=None):
            b = take(pe, key)
            for k in range(K):
                if pre is not None:
                    pe.wait_ge(h_ready.sem, pre.h + (k + 1) * pre.halves)
                mm(ps[0:M, b, 0:T], w[:, k, col:col + M], H_[:, k, 0:T], k == 0, k == K - 1,
                   b if k == K - 1 else None)

        class Chain:

            def __init__(self, eng, own):
                self.eng, self.own, self.n = eng, own, 0

            def step(self, ins):
                self.n += 1
                ins.then_inc(self.own, 1)
                self.eng.wait_ge(self.own, self.n)

            def mark(self, ins, sig, value):
                s = sig.sem if isinstance(sig, Signal) else sig
                ins.then_inc(s, 1)
                self.eng.wait_ge(s, value)

            def free(self, ins, key):
                b, use = place[key]
                ins.then_inc(bank_free[b], 1)
                self.eng.wait_ge(bank_free[b], use)

        V = nc.vector
        S = nc.scalar

        vec_ready = sem("vec_ready")

        def pe_vectors(pe):
            pe.wait_ge(small_loaded, SMALL)
            for i in range(3):
                b = take(pe, ("vec", i))
                nc.tensor.transpose(ps[:, b, 0:P], VROW[:, i, :], ident).then_inc(bank_full[b], 1)

        def dve_vectors(c):
            c.step(V.memset(SC[:], 0.0))
            for i in range(3):
                b = full_of(c.eng, ("vec", i))
                c.free(V.tensor_copy(VEC[:, i * P:(i + 1) * P], ps[:, b, 0:P]), ("vec", i))
            c.eng.wait_ge(side_loaded, 48)
            for i in range(2):
                c.step(V.tensor_tensor(LV[:, 2 * i, :], LV[:, 2 * i, :], LV[:, 2 * i + 1, :], ALU.mult))
                c.step(V.reduce_sum(LAM[:, i:i + 1], LV[:, 2 * i, :], axis=AX_X))
            l0 = vec("lb", 0, 16).rearrange("p (d t h) -> p d t h", d=2, t=2)
            lo = [LB[:, i, :].rearrange("p (d h) -> p d h", d=2) for i in range(6)]
            c.step(V.tensor_tensor(lo[0], l0[:, :, 0, :], l0[:, :, 1, :], ALU.max))
            c.step(V.tensor_tensor(lo[1], l0[:, :, 0, :], lo[0], ALU.subtract))
            c.step(V.tensor_tensor(lo[2], l0[:, :, 1, :], lo[0], ALU.subtract))
            ins = V.tensor_scalar(LAM[:, 4:5], vec("subln"), 1.0 - LAM_INIT, None, ALU.mult)
            ins.then_inc(vec_ready, 1)

        def act_cond(c):
            c.eng.wait_ge(vec_ready, 1)
            for i, n in enumerate(("c", "c_ctx", "c_2", "c_ctx_2")):
                c.step(S.activation(SC[:, :, i // 2, i % 2], vec(n, 0, 8), ACT.Silu))
            c.step(S.activation(LAM[:, 2:4], LAM[:, 0:2], ACT.Exp))
            S.activation(LB[:, 1:3, :], LB[:, 1:3, :], ACT.Exp).then_inc(cond_ready, 1)

        def dve_small(c):
            c.eng.wait_ge(cond_ready, 1)
            c.step(V.tensor_tensor(LAM[:, 5:6], LAM[:, 3:4], LAM[:, 2:3], ALU.subtract))
            c.step(V.tensor_scalar(LAM[:, 6:7], LAM[:, 5:6], LAM_INIT, None, ALU.subtract))
            c.step(V.tensor_copy(MASK[:], MASKF))
            c.step(V.tensor_tensor(LB[:, 3, :], LB[:, 1, :], LB[:, 2, :], ALU.add))
            c.step(V.reciprocal(LB[:, 4, :], LB[:, 3, :]))
            c.step(V.tensor_tensor(LB[:, 0, :], LB[:, 1, :], LB[:, 4, :], ALU.mult))
            c.step(V.tensor_scalar(LB[:, 5, :], LB[:, 0, :], -1.0, 1.0, ALU.mult, ALU.add))

        ADA = ar(9728, 3, 512)

        def pe_ada_job(pe, l, n):
            g, i = n // 4, n % 4
            if i == 0:
                take(pe, ("ada", l, g), fixed=l > 0)
            b = place[("ada", l, g)][0]
            w = weights(pe, ("ada", l, n)).rearrange("p (k n) -> p k n", k=2)
            for kk in range(2):
                k = 2 * i + kk
                for j in range(4):
                    mm(ps[32 * j:32 * j + 32, b, :], SC[:, k, l // 2, :], w[:, kk, j * 512:(j + 1) * 512],
                       k == 0, k == 7, b if k == 7 and j == 3 else None)
            used()

        def pe_ada_turn(pe, l, g):
            b = take(pe, ("adaT", l, g))
            freed(pe, ("ada", l, g))
            for i in range(4):
                m = nc.tensor.transpose(ps[:, b, i * P:(i + 1) * P], ADA[:, g, i * P:(i + 1) * P], ident)
            m.then_inc(bank_full[b], 1)

        def dve_ada_rows(c, l, g):
            b = full_of(c.eng, ("ada", l, g))
            c.free(V.tensor_copy(ADA[:, g, :], ps[:, b, :]), ("ada", l, g))

        def dve_ada_turned(c, l, g):
            b = full_of(c.eng, ("adaT", l, g))
            src = ps[:, b, :].rearrange("p (i j s) -> p j i s", i=4, j=4)[:, :, :, 0:2]
            dst = MOD[:, l, 16 * g:16 * g + 16, :].rearrange("p (j i) s -> p j i s", j=4)
            c.free(V.tensor_copy(dst, src), ("adaT", l, g))

        def dve_mods(c, l):
            bias = vec(f"ada_b{l}", 0, 48).unsqueeze(2).broadcast_to([P, 48, 2])
            c.step(V.tensor_tensor(MOD[:, l, :, :], MOD[:, l, :, :], bias, ALU.add))
            for w in range(2):
                g = vec("norm_g", (l * 4 + 2 * w) * 8, 8) if l < 2 else vec(("norm_mix", "norm_ffn")[w], 0, 8)
                c.step(V.scalar_tensor_tensor(out=AMP[:, l, w, :, :], in0=MOD[:, l, 24 * w + 8:24 * w + 16, :],
                                              scalar=1.0, in1=g.unsqueeze(2).broadcast_to([P, 8, 2]),
                                              op0=ALU.add, op1=ALU.mult))
                if l < 2:
                    g = vec("norm_g", (l * 4 + 2 * w + 1) * 8, 8).unsqueeze(2).broadcast_to([P, 8, 2])
                    c.step(V.tensor_tensor(GATE[:, l, w, :, :], MOD[:, l, 24 * w + 16:24 * w + 24, :], g, ALU.mult))

        def pe_adaln0(pe):
            pe.wait_ge(cond_ready, 1)
            for n in range(12):
                pe_ada_job(pe, 0, n)
            for g in range(3):
                pe_ada_turn(pe, 0, g)

        def dve_adaln0(c):
            for g in range(3):
                dve_ada_rows(c, 0, g)
            for g in range(3):
                dve_ada_turned(c, 0, g)
            dve_mods(c, 0)

        def pe_ada_beside(pe, i):
            n, G = i // 2, (i - 9) // 8
            if i % 8 == 1 and 0 <= G < 6:
                pe_ada_turn(pe, 1 + G // 3, G % 3)
            if i % 2 and n < 24:
                pe_ada_job(pe, 1 + n // 12, n % 12)

        def dve_ada_beside(c, i):
            G = (i - 8) // 8
            if i % 8 == 0 and 0 <= G < 6:
                dve_ada_rows(c, 1 + G // 3, G % 3)
            G = (i - 10) // 8
            if i % 8 == 2 and 0 <= G < 6:
                dve_ada_turned(c, 1 + G // 3, G % 3)

        def pe_load(pe, name, stage, tcs, ready):
            ready(pe)
            for k in range(KD):
                b = take(pe, (name, k))
                for t in range(tcs):
                    m = nc.tensor.transpose(ps[:, b, t * P:(t + 1) * P], stage[:, t, k * P:(k + 1) * P], ident)
                m.then_inc(bank_full[b], 1)

        def dve_load(c, name, t0, T):
            for k in range(KD):
                b = full_of(c.eng, (name, k))
                c.free(V.tensor_copy(X[:, k, t0:t0 + T], ps[:, b, 0:T]), (name, k))

        def act_squares(c, base, chunks, src, sq, wait):
            for k in range(chunks):
                wait(c.eng, k)
                c.mark(S.activation(sq(k), src(k), ACT.Square), squares_ready, base + k + 1)

        def pe_sums(pe, key, chunks, sq, T, wait):
            b = take(pe, key)
            for k in range(chunks):
                wait(pe, k)
                mm(ps[:, b, 0:T], ones, sq(k), k == 0, k == chunks - 1, b if k == chunks - 1 else None)

        def act_rstd(c, key, base, width, T, dst):
            b = full_of(c.eng, key)
            c.free(S.activation(dst, ps[:, b, 0:T], ACT.Ln, scale=1.0 / width, bias=ft("eps")), key)
            c.mark(S.activation(dst, dst, ACT.Exp, scale=-0.5), rstd_ready, base + 1)

        class Pre:

            def __init__(self, name, l, w, halves):
                self.name, self.l, self.w, self.halves, self.T = name, l, w, halves, TX * halves
                self.sq = squares_ready.plan(KD)
                self.rs = rstd_ready.plan(1)
                self.sc = scaled_ready.plan(KD * halves)
                self.h = h_ready.plan(KD * halves)

            def squares(self, k):
                return H[:, k, 0:self.T]

            def act(self, c, wait):
                act_squares(c, self.sq, KD, lambda k: X[:, k, 0:self.T], self.squares, wait)
                act_rstd(c, ("sum", self.name), self.rs, D, self.T, RS[:, 0:self.T])
                for k in range(KD):
                    for h in range(self.halves):
                        n = k * self.halves + h
                        t = slice(h * TX, (h + 1) * TX)
                        c.eng.wait_ge(scaled_ready.sem, self.sc + n + 1)
                        c.mark(S.activation(H[:, k, t], H[:, k, t], ACT.Identity,
                                              bias=MOD[:, self.l, 24 * self.w + k, h:h + 1]), h_ready, self.h + n + 1)

            def pe(self, pe):
                pe_sums(pe, ("sum", self.name), KD, self.squares, self.T,
                        lambda e, k: e.wait_ge(squares_ready.sem, self.sq + k + 1))

            def ready(self, pe):
                pe.wait_ge(h_ready.sem, self.h + KD * self.halves)

            def dve(self, c):
                c.eng.wait_ge(rstd_ready.sem, self.rs + 1)
                for k in range(KD):
                    for h in range(self.halves):
                        t = slice(h * TX, (h + 1) * TX)
                        c.mark(V.scalar_tensor_tensor(out=H[:, k, t], in0=X[:, k, t],
                                                        scalar=AMP[:, self.l, self.w, k, h:h + 1], in1=RS[:, t],
                                                        op0=ALU.mult, op1=ALU.mult),
                                 scaled_ready, self.sc + k * self.halves + h + 1)

        class Post:

            def __init__(self, name, l, w, halves, Y, SQ):
                self.name, self.l, self.w, self.halves, self.T, self.Y, self.SQ = name, l, w, halves, TX * halves, Y, SQ
                self.rs = rstd_ready.plan(1)
                self.x = x_ready.plan(KD)

            def act(self, c):
                for k in range(KD):
                    b = full_of(c.eng, (self.name, k))
                    c.step(S.activation(self.Y(k), ps[:, b, 0:self.T], ACT.Copy))
                    c.free(S.activation(self.SQ(k), ps[:, b, 0:self.T], ACT.Square), (self.name, k))
                act_rstd(c, ("sum", self.name), self.rs, D, self.T, RS[:, 0:self.T])

            def pe(self, pe):
                pe_sums(pe, ("sum", self.name), KD, self.SQ, self.T, lambda e, k: freed(e, (self.name, k)))

            def dve(self, c):
                c.eng.wait_ge(rstd_ready.sem, self.rs + 1)
                for k in range(KD):
                    for h in range(self.halves):
                        t = slice(h * TX, (h + 1) * TX)
                        c.step(V.scalar_tensor_tensor(out=self.Y(k)[:, t], in0=self.Y(k)[:, t],
                                                      scalar=GATE[:, self.l, self.w, k, h:h + 1], in1=RS[:, t],
                                                      op0=ALU.mult, op1=ALU.mult))
                    c.mark(V.tensor_tensor(X[:, k, 0:self.T], X[:, k, 0:self.T], self.Y(k), ALU.add),
                             x_ready, self.x + k + 1)

        PR = ar(12288, 2, 2, 512)
        PT = ar(14336, 2, 4, P)

        class Unit:
            def __init__(self, key, maps, nk, scale, vals, dv, out, mask=None, sink=None):
                self.key, self.maps, self.nk, self.scale, self.vals = key, maps, nk, scale, vals
                self.dv, self.out, self.mask, self.sink = dv, out, mask, sink

        class Attention:
            def __init__(self, units, pe_beside=None, dve_beside=None):
                self.units, self.pe_beside, self.dve_beside = units, pe_beside, dve_beside
                self.stat = stat_ready.plan(len(units))
                self.prob = probs_ready.plan(len(units))

            def pe_scores(self, pe, i):
                u = self.units[i]
                for m, (q, k) in enumerate(u.maps):
                    b = take(pe, ("s", u.key, m))
                    mm(ps[:, b, 0:u.nk], q, k, True, True, b)

            def pe(self, pe):
                n = len(self.units)
                for i in range(min(3, n)):
                    self.pe_scores(pe, i)
                for i, u in enumerate(self.units):
                    kc = u.nk // P
                    b = take(pe, ("t", u.key))
                    pe.wait_ge(probs_ready.sem, self.prob + i + 1)
                    for j in range(kc):
                        m = nc.tensor.transpose(ps[:, b, j * P:(j + 1) * P], PR[:, i % 2, 0, j * P:(j + 1) * P], ident)
                    m.then_inc(bank_full[b], 1)
                    if i + 3 < n:
                        self.pe_scores(pe, i + 3)
                    b = take(pe, ("o", u.key))
                    freed(pe, ("t", u.key))
                    o = u.out[0]
                    for j in range(kc):
                        mm(ps[o:o + u.dv, b, 0:P], u.vals[j], PT[:, i % 2, j, :], j == 0, j == kc - 1,
                           b if j == kc - 1 else None)
                    if self.pe_beside:
                        self.pe_beside(pe, i)

            def dve_stats(self, c, i):
                u = self.units[i]
                st = ST[:, i % 2, :]
                for m in range(len(u.maps)):
                    b = full_of(c.eng, ("s", u.key, m))
                    if u.mask is not None:
                        c.step(V.tensor_tensor(ps[:, b, 0:TX], ps[:, b, 0:TX], u.mask, ALU.add))
                    c.step(V.reduce_max(st[:, m:m + 1], ps[:, b, 0:u.nk], axis=AX_X))
                n = len(u.maps)
                if u.sink is not None:
                    c.step(V.tensor_scalar(st[:, 0:1], st[:, 0:1], u.scale, u.sink, ALU.mult, ALU.max))
                    ins = V.tensor_scalar(st[:, 2:3], st[:, 0:1], -1.0, None, ALU.mult)
                else:
                    ins = V.tensor_scalar(st[:, 2:2 + n], st[:, 0:n], -u.scale, None, ALU.mult)
                c.mark(ins, stat_ready, self.stat + i + 1)

            def act_exp(self, c, i):
                u = self.units[i]
                st = ST[:, i % 2, :]
                c.eng.wait_ge(stat_ready.sem, self.stat + i + 1)
                if i >= 2:
                    full_of(c.eng, ("t", self.units[i - 2].key))
                if u.sink is not None:
                    c.step(S.activation(st[:, 5:6], u.sink, ACT.Exp, bias=st[:, 2:3]))
                for m in range(len(u.maps)):
                    b = place[("s", u.key, m)][0]
                    c.free(S.activation(PR[:, i % 2, m, 0:u.nk], ps[:, b, 0:u.nk], ACT.Exp, bias=st[:, 2 + m:3 + m],
                                        scale=u.scale, accum_out=st[:, 6 + m:7 + m]), ("s", u.key, m))

            def act(self, c):
                n = len(self.units)
                for i in range(min(2, n)):
                    self.act_exp(c, i)
                for i, u in enumerate(self.units):
                    b = full_of(c.eng, ("t", u.key))
                    if i >= 2:
                        full_of(c.eng, ("o", self.units[i - 2].key))
                    dst = PT[:, i % 2, 0:u.nk // P, :].rearrange("p a b -> p (a b)")
                    c.free(S.activation(dst, ps[:, b, 0:u.nk], ACT.Copy), ("t", u.key))
                    if i + 2 < n:
                        self.act_exp(c, i + 2)

            def dve_probs(self, c, i):
                u = self.units[i]
                st = ST[:, i % 2, :]
                n = len(u.maps)
                for m in range(n):
                    freed(c.eng, ("s", u.key, m))
                if u.sink is not None:
                    c.step(V.tensor_tensor(st[:, 6:7], st[:, 6:7], st[:, 5:6], ALU.add))
                c.step(V.reciprocal(st[:, 3:3 + n], st[:, 6:6 + n]))
                p0 = PR[:, i % 2, 0, 0:u.nk]
                ins = V.tensor_scalar(p0, p0, st[:, 3:4], None, ALU.mult)
                if n == 2:
                    c.step(ins)
                    c.step(V.tensor_tensor(st[:, 4:5], st[:, 4:5], LAM[:, 6:7], ALU.mult))
                    ins = V.scalar_tensor_tensor(out=p0, in0=PR[:, i % 2, 1, 0:u.nk], scalar=st[:, 4:5], in1=p0,
                                                 op0=ALU.mult, op1=ALU.add)
                c.mark(ins, probs_ready, self.prob + i + 1)

            def dve_out(self, c, i):
                u = self.units[i]
                b = full_of(c.eng, ("o", u.key))
                o = u.out[0]
                c.free(V.tensor_copy(u.out[1], ps[o:o + u.dv, b, 0:P]), ("o", u.key))

            def dve(self, c):
                n = len(self.units)
                for i in range(min(2, n)):
                    self.dve_stats(c, i)
                for i in range(n):
                    self.dve_probs(c, i)
                    if i + 2 < n:
                        self.dve_stats(c, i + 2)
                    if i >= 1:
                        self.dve_out(c, i - 1)
                    if self.dve_beside:
                        self.dve_beside(c, i)
                self.dve_out(c, n - 1)

        HID = ar(0, KF, T2)
        TG = ar(11264, 2, 512)

        def pe_ffn(pe, l, T, pre):
            hid = HID if T == T2 else ar(0, KF, TX)
            for i in range(KF // 2):
                w = weights(pe, ("w13", l, i)).rearrange("p (k n) -> p k n", k=KD)
                for j in range(2):
                    pe_dense(pe, ("g", l, 2 * i + j), w, j * P, H, T, pre=pre if i + j == 0 else None)
                    pe_dense(pe, ("u", l, 2 * i + j), w, 256 + j * P, H, T)
                used()
            freed(pe, ("u", l, KF - 1))
            for n in range(KD):
                w = weights(pe, ("w2", l, n))[:, 0:KF * P].rearrange("p (k n) -> p k n", k=KF)
                pe_dense(pe, (("ffn", l), n), w, 0, hid, T, K=KF)
                used()

        def act_ffn(c, l, T):
            for j in range(KF):
                b = full_of(c.eng, ("g", l, j))
                if j >= 2:
                    freed(c.eng, ("u", l, j - 2))
                c.free(S.activation(TG[:, j % 2, 0:T], ps[:, b, 0:T], ACT.Silu), ("g", l, j))

        def dve_ffn(c, l, T):
            hid = HID if T == T2 else ar(0, KF, TX)
            for j in range(KF):
                freed(c.eng, ("g", l, j))
                b = full_of(c.eng, ("u", l, j))
                c.free(V.tensor_tensor(hid[:, j, 0:T], TG[:, j % 2, 0:T], ps[:, b, 0:T], ALU.mult), ("u", l, j))

        QK = ar(0, 14, T2)
        VA = ar(7168, 4, P)
        VB = ar(7680, 4, 512)
        TMP = ar(15104, TX)
        AB_CHUNKS = ([(0, j, j) for j in range(4)] + [(1, j, 6 + j) for j in range(4)] + [(2, 0, 4)]
                     + [(3, j, 10 + j) for j in range(4)])
        ROPED = [c for _, _, c in AB_CHUNKS[:9]] + [5] + [c for _, _, c in AB_CHUNKS[9:]]
        rope_base = roped.plan(len(ROPED))

        def pe_ab_in(pe, pre):
            turn = []

            def rotate(cq):
                b = take(pe, ("rot", cq))
                freed(pe, ("qk", cq))
                mm(ps[:, b, 0:TX], ft("perm_ab"), QK[:, cq, 0:TX], True, True, b)

            for jb in range(5):
                n = AB_COLS[jb][1] - AB_COLS[jb][0]
                w = weights(pe, ("ab_in", jb))[:, 0:KD * n].rearrange("p (k n) -> p k n", k=KD)
                for jj, col, cq in AB_CHUNKS:
                    if jj == jb:
                        pe_dense(pe, ("qk", cq), w, col * P, H, T2, pre=pre if cq == 0 else None)
                        turn.append(cq)
                        if len(turn) > 1:
                            rotate(turn.pop(0))
                        if cq == 4:
                            place[("qk", 5)] = place[("qk", 4)]
                            turn.append(5)
                if jb in (2, 4):
                    for t in range(4):
                        b = take(pe, ("v", jb, t))
                        width, c0 = (P, P) if jb == 2 else (512, 0)
                        for k in range(KD):
                            mm(ps[:, b, 0:width], H[:, k, t * P:(t + 1) * P], w[:, k, c0:c0 + width], k == 0,
                               k == KD - 1, b if k == KD - 1 else None)
                if jb in (2, 3):
                    while turn:
                        rotate(turn.pop(0))
                used()

        def act_ab_in(c):
            for jb in range(5):
                for jj, col, cq in AB_CHUNKS:
                    if jj == jb and cq != 4:
                        b = full_of(c.eng, ("qk", cq))
                        c.free(S.activation(QK[:, cq, :], ps[:, b, :], ACT.Copy), ("qk", cq))
                if jb in (2, 4):
                    for t in range(4):
                        b = full_of(c.eng, ("v", jb, t))
                        dst, width = (VA[:, t, :], P) if jb == 2 else (VB[:, t, :], 512)
                        c.free(S.activation(dst, ps[:, b, 0:width], ACT.Copy), ("v", jb, t))

        def dve_rope(c, i, dst, key, tmp, cos, sin, rows=P):
            b = full_of(c.eng, key)
            n = int(np.prod(dst.shape[1:]))
            rot = ps[0:rows, b, 0:n]
            if len(dst.shape) == 3:
                rot = rot.rearrange("p (a b) -> p a b", a=dst.shape[1])
            c.free(V.tensor_tensor(tmp, rot, sin, ALU.mult), key)
            c.step(V.tensor_tensor(dst, dst, cos, ALU.mult))
            c.mark(V.tensor_tensor(dst, dst, tmp, ALU.add), roped, i + 1)

        def dve_ab_in(c):
            for i, cq in enumerate(ROPED):
                if cq == 4:
                    b = full_of(c.eng, ("qk", 4))
                    for g in range(2):
                        for h in range(2):
                            ins = V.tensor_copy(QK[64 * h:64 * h + 64, 4 + g, :], ps[64 * g:64 * g + 64, b, :])
                            (c.free(ins, ("qk", 4)) if g + h == 2 else c.step(ins))
                dve_rope(c, rope_base + i, QK[:, cq, 0:TX], ("rot", cq), TMP, ft("cos_ab"), ft("sin_ab"))

        ab_units = []
        for h in range(AH):
            for qc in range(4):
                r = slice(64 * (h % 2), 64 * (h % 2) + 64)
                k0 = 0 if qc < 2 else TX
                q = QK[r, h // 2, qc * P:(qc + 1) * P]
                k = QK[r, 4 + h // 4, k0:T2]
                g = h // 4
                vals = [VA[:, t, g * 64:(g + 1) * 64] for t in range(k0 // P, 4)]
                mask = ft("window")[:, qc * TX:(qc + 1) * TX] if qc < 2 else None
                ab_units.append(Unit(("a", h, qc), [(q, k)], T2 - k0, DH ** -0.5, vals, 64,
                                     (64 * (h % 2), H[r, h // 2, qc * P:(qc + 1) * P]), mask, SINK[:, h:h + 1]))
        for h in range(BH):
            for qc in range(4):
                k0 = 0 if qc < 2 else TX
                maps = [(QK[64 * m:64 * m + 64, 6 + h, qc * P:(qc + 1) * P], QK[64 * m:64 * m + 64, 10 + h, k0:T2])
                        for m in range(2)]
                vals = [VB[:, t, h * P:(h + 1) * P] for t in range(k0 // P, 4)]
                ab_units.append(Unit(("b", h, qc), maps, T2 - k0, DH ** -0.5, vals, P,
                                     (0, H[:, 4 + h, qc * P:(qc + 1) * P])))

        SUB_SQ, SUB_RS = ar(0, 4, T2), ar(2048, 4, T2)

        def pe_subln(pe):
            for h in range(BH):
                pe_sums(pe, ("sub", h), 1, lambda k: SUB_SQ[:, h, :], T2,
                        lambda e, k: e.wait_ge(squares_ready.sem, sub_sq + h + 1))

        def act_subln(c):
            freed(c.eng, ("o", ("b", BH - 1, 3)))
            act_squares(c, sub_sq, BH, lambda h: H[:, 4 + h, :], lambda h: SUB_SQ[:, h, :], lambda e, k: None)
            for h in range(BH):
                act_rstd(c, ("sub", h), sub_rs + h, BV, T2, SUB_RS[:, h, :])

        def dve_subln(c):
            for h in range(BH):
                c.eng.wait_ge(rstd_ready.sem, sub_rs + h + 1)
                c.mark(V.scalar_tensor_tensor(out=H[:, 4 + h, :], in0=H[:, 4 + h, :], scalar=LAM[:, 4:5],
                                                in1=SUB_RS[:, h, :], op0=ALU.mult, op1=ALU.mult), o_ready, sub_o + h + 1)

        def pe_out(pe, name, label, Hf, T, wait):
            wait(pe)
            for i in range(2):
                w = weights(pe, (label, i)).rearrange("p (k n) -> p k n", k=KD)
                for j in range(4):
                    b = take(pe, (name, 4 * i + j))
                    for k in range(KD):
                        mm(ps[:, b, 0:T], w[:, k, j * P:(j + 1) * P], Hf(k), k == 0, k == KD - 1,
                           b if k == KD - 1 else None)
                used()

        KM = ar(0, CH, T2)
        VM = ar(8192, 4, CH * CV)
        QM = H[:].rearrange("p k (a t) -> p (k a) t", a=2)
        KR = ar(12288, T2)
        LSQ = ar(8192, 7, TX)
        RSK = ar(12800, T2)
        MT = ar(13312, 2, TX)

        def lat(i):
            return X[:, i, TX:T2]

        def lat_kv(c):
            return X[:, 3 + 2 * c:5 + 2 * c, TX:T2]

        def pe_mla_in(pe, pre):
            w = weights(pe, "mla_q")[:, 0:KD * QL].rearrange("p (k n) -> p k n", k=KD)
            for j in range(3):
                pe_dense(pe, ("lq", j), w, j * P, H, TX, pre=pre if j == 0 else None)
            used()
            n = KVL + ROPE
            w = weights(pe, "mla_kv")[:, 0:KD * n].rearrange("p (k n) -> p k n", k=KD)
            for j in range(2):
                pe_dense(pe, ("lk", j), w, j * P, H, T2)
            pe_dense(pe, "kr", w, n - CQK, H, T2, M=CQK)
            used()
            pe_sums(pe, "sum_lq", 3, lambda k: LSQ[:, k, :], TX, lambda e, k: freed(e, ("lq", k)))
            b = take(pe, "rot_kr")
            freed(pe, "kr")
            mm(ps[0:CQK, b, 0:TX], ft("perm_c", CQK, CQK), KR[0:CQK, 0:TX], True, True, b)
            pe_sums(pe, "sum_lk", 2, lambda k: LSQ[:, 3 + 2 * k:5 + 2 * k, :].rearrange("p a b -> p (a b)"), T2,
                    lambda e, k: freed(e, ("lk", k)))
            pe.wait_ge(lat_ready.sem, 3)

            def rotate(i):
                b = take(pe, ("rotm", i))
                freed(pe, ("qm", i))
                for a in range(2):
                    mm(ps[0:CQK, b, a * TX:(a + 1) * TX], ft("perm_c", CQK, CQK), QM[0:CQK, 2 * i + a, :], True, True,
                       b if a else None)

            for i in range(8):
                if i % 4 == 0:
                    w = weights(pe, ("wq_b", i // 4))[:, 0:3 * 768].rearrange("p (k n) -> p k n", k=3)
                b = take(pe, ("qm", i))
                for a in range(2):
                    for k in range(3):
                        col = (2 * (i % 4) + a) * CQK
                        mm(ps[0:CQK, b, a * TX:(a + 1) * TX], w[:, k, col:col + CQK], lat(k), k == 0, k == 2,
                           b if a and k == 2 else None)
                if i % 4 == 3:
                    used()
                if i:
                    rotate(i - 1)
            rotate(7)
            pe.wait_ge(lat_ready.sem, 5)
            w = weights(pe, "wkv_b").rearrange("p (k n) -> p k n", k=2)
            for h in range(CH):
                b = take(pe, ("km", h))
                for k in range(2):
                    mm(ps[0:64, b, :].rearrange("p (a b) -> p a b", a=2), w[:, k, h * P:h * P + 64], lat_kv(k), k == 0,
                       k == 1, b if k else None)
            for t in range(4):
                for g in range(2):
                    b = take(pe, ("vm", t, g))
                    for k in range(2):
                        v = w[:, k, :].rearrange("p (h c) -> p h c", h=CH)[:, 8 * g:8 * g + 8, 64:128]
                        x = X[:, 3 + 2 * k + t // 2, TX + (t % 2) * P:TX + (t % 2 + 1) * P]
                        mm(ps[:, b, :].rearrange("p (h c) -> p h c", h=8), x, v, k == 0, k == 1, b if k else None)
            used()

        def act_mla_in(c):
            for j in range(3):
                b = full_of(c.eng, ("lq", j))
                c.step(S.activation(lat(j), ps[:, b, 0:TX], ACT.Copy))
                c.free(S.activation(LSQ[:, j, :], ps[:, b, 0:TX], ACT.Square), ("lq", j))
            for j in range(2):
                b = full_of(c.eng, ("lk", j))
                two = ps[:, b, :].rearrange("p (a b) -> p a b", a=2)
                c.step(S.activation(lat_kv(j), two, ACT.Copy))
                c.free(S.activation(LSQ[:, 3 + 2 * j:5 + 2 * j, :], two, ACT.Square), ("lk", j))
            b = full_of(c.eng, "kr")
            c.free(S.activation(KR[0:CQK, :], ps[0:CQK, b, :], ACT.Copy), "kr")
            act_rstd(c, "sum_lq", lat_rs, QL, TX, RS[:, 0:TX])
            act_rstd(c, "sum_lk", lat_rs + 1, KVL, T2, RSK)
            for i in range(8):
                b = full_of(c.eng, ("qm", i))
                c.free(S.activation(QM[0:CQK, 2 * i:2 * i + 2, :], ps[0:CQK, b, :].rearrange("p (a b) -> p a b", a=2),
                                    ACT.Copy), ("qm", i))
            for h in range(0, CH):
                b = full_of(c.eng, ("km", h))
                c.free(S.activation(KM[0:64, h, :], ps[0:64, b, :], ACT.Copy), ("km", h))

        def dve_mla_in(c):
            c.eng.wait_ge(rstd_ready.sem, lat_rs + 1)
            for j in range(3):
                c.mark(V.scalar_tensor_tensor(out=lat(j), in0=lat(j), scalar=vec("q_norm", j), in1=RS[:, 0:TX],
                                                op0=ALU.mult, op1=ALU.mult), lat_ready, j + 1)
            dve_rope(c, krope, KR[0:CQK, 0:TX], "rot_kr", MT[0:CQK, 0, :], ft("cos_c", p=CQK), ft("sin_c", p=CQK), CQK)
            c.eng.wait_ge(rstd_ready.sem, lat_rs + 2)
            for j in range(2):
                c.mark(V.scalar_tensor_tensor(out=lat_kv(j), in0=lat_kv(j), scalar=vec("kv_norm", j),
                                                in1=RSK.rearrange("p (a b) -> p a b", a=2),
                                                op0=ALU.mult, op1=ALU.mult), lat_ready, 4 + j)
            c.step(V.tensor_copy(KM[64:96, :, :], KR[64:96, :].unsqueeze(1).broadcast_to([32, CH, T2])))
            for i in range(8):
                two = [CQK, 2, TX]
                dve_rope(c, qrope + i, QM[0:CQK, 2 * i:2 * i + 2, :], ("rotm", i), MT[0:CQK, :, :],
                         ft("cos_c", p=CQK).unsqueeze(1).broadcast_to(two),
                         ft("sin_c", p=CQK).unsqueeze(1).broadcast_to(two), CQK)
            for t in range(4):
                for g in range(2):
                    b = full_of(c.eng, ("vm", t, g))
                    c.free(V.tensor_copy(VM[:, t, g * 512:(g + 1) * 512], ps[:, b, :]), ("vm", t, g))

        mla_units = []
        for h in range(CH):
            for qc in range(2):
                o = 64 * (h % 2)
                mla_units.append(Unit(("m", h, qc), [(QM[0:CQK, h, qc * P:(qc + 1) * P], KM[0:CQK, h, :])], T2,
                                      CQK ** -0.5, [VM[:, t, h * CV:(h + 1) * CV] for t in range(4)], CV,
                                      (o, KM[o:o + CV, 2 * (h // 2), qc * P:(qc + 1) * P])))

        FG = [ar(0, HH, T2), ar(2048, HH, T2)]
        V2 = ar(4096, 4, HW_)
        Q2 = ar(6144, HH, TX)
        BC = [ar(7168, HH, T2), ar(9216, HH, T2)]
        E_, QE, KE = ar(11264, HH, TX), ar(12288, HH, TX), ar(13312, HH, TX)
        STATE = ar(14336, 2, HH, P)
        O2 = ar(11264, HH, TX)
        GR = ar(12288, HH, TX)

        def score_t(jc):
            return FG[jc][:, :, TX:T2]

        LEV = [(s, d) for s in [P] + LEVELS for d in range(2)]

        def pe_hgrn_in(pe, pre):
            for d in range(2):
                w = weights(pe, ("in2", d)).rearrange("p (k n) -> p k n", k=KD)
                for h in range(HH):
                    pe_dense(pe, ("fz", d, h), w, h * P, H, T2, pre=pre if d + h == 0 else None)
                used()
            w = weights(pe, ("in2", 2)).rearrange("p (k n) -> p k n", k=KD)
            for t in range(4):
                b = take(pe, ("v2", t))
                for k in range(KD):
                    mm(ps[:, b, :], H[:, k, t * P:(t + 1) * P], w[:, k, :], k == 0, k == KD - 1, b if k == KD - 1 else None)
            used()
            w = weights(pe, ("in2", 3)).rearrange("p (k n) -> p k n", k=KD)
            for h in range(HH):
                pe_dense(pe, ("q2", h), w, h * P, H, TX)
            used()

        def act_hgrn_in(c):
            for d in range(2):
                for h in range(HH):
                    b = full_of(c.eng, ("fz", d, h))
                    c.free(S.activation(FG[d][:, h, :], ps[:, b, :], ACT.Sigmoid), ("fz", d, h))
            for t in range(4):
                b = full_of(c.eng, ("v2", t))
                c.free(S.activation(V2[:, t, :], ps[:, b, :], ACT.Copy), ("v2", t))
            for h in range(HH):
                b = full_of(c.eng, ("q2", h))
                c.free(S.activation(Q2[:, h, :], ps[:, b, 0:TX], ACT.Silu), ("q2", h))
            for d in range(2):
                for h in range(HH):
                    c.eng.wait_ge(fg_ready, 4 * d + h + 1)
                    c.mark(S.activation(BC[d][:, h, :], FG[d][:, h, :], ACT.Ln), logf_ready, 4 * d + h + 1)
            for d in range(2):
                c.eng.wait_ge(sums_ready, 4 * d + 4)
                if d:
                    c.eng.wait_ge(kw_ready, 1)
                for h in range(HH):
                    end = BC[d][:, h, T2 - 1:T2] if d == 0 else BC[d][:, h, TX:TX + 1]
                    ins = S.activation(E_[:, h, :], BC[d][:, h, TX:T2], ACT.Exp, scale=-1.0, bias=end)
                    c.mark(ins, left_ready, 4 * d + h + 1)

        def dve_hgrn_in(c):
            for d in range(2):
                for h in range(HH):
                    freed(c.eng, ("fz", d, h))
                    i = 4 * d + h
                    c.mark(V.tensor_scalar(FG[d][:, h, :], FG[d][:, h, :], LB[:, 5, i:i + 1], LB[:, 0, i:i + 1],
                                             ALU.mult, ALU.add), fg_ready, i + 1)
            one = ft("ones", 1).broadcast_to([P, TX])
            for d in range(2):
                for h in range(HH):
                    c.eng.wait_ge(logf_ready.sem, 4 * d + h + 1)
                    c.step(V.tensor_scalar(FG[d][:, h, :], FG[d][:, h, :], -1.0, 1.0, ALU.mult, ALU.add))
                    for half in range(2):
                        v = BC[d][:, h, half * TX:(half + 1) * TX]
                        if d:
                            v = v[:, ::-1]
                        ins = V.tensor_tensor_scan(v, one, v, 0.0, ALU.mult, ALU.add)
                        (c.mark(ins, sums_ready, 4 * d + h + 1) if half else c.step(ins))
            for d in range(2):
                c.eng.wait_ge(left_ready, 4 * d + 4)
                if d:
                    full_of(c.eng, ("kwt", 0, 1))
                c.mark(V.tensor_tensor(QE[:], FG[d][:, :, TX:T2], E_[:], ALU.mult), kw_ready, d + 1)
                for t in range(2):
                    b = full_of(c.eng, ("kwt", d, t))
                    dst = BC[d][:, :, TX + t * P:TX + (t + 1) * P]
                    c.free(V.tensor_copy(dst, ps[:, b, :].rearrange("p (h k) -> p h k", h=HH)), ("kwt", d, t))
                b = full_of(c.eng, ("state", d))
                c.free(V.tensor_copy(STATE[:, d, :, :], ps[:, b, :].rearrange("p (h k) -> p h k", h=HH)), ("state", d))

        def pe_hgrn_state(pe):
            for d in range(2):
                pe.wait_ge(kw_ready, d + 1)
                for t in range(2):
                    b = take(pe, ("kwt", d, t))
                    for h in range(HH):
                        m = nc.tensor.transpose(ps[:, b, h * P:(h + 1) * P], QE[:, h, t * P:(t + 1) * P], ident)
                    m.then_inc(bank_full[b], 1)
                b = take(pe, ("state", d))
                for t in range(2):
                    freed(pe, ("kwt", d, t))
                for h in range(HH):
                    for t in range(2):
                        mm(ps[:, b, h * P:(h + 1) * P], BC[d][:, h, TX + t * P:TX + (t + 1) * P],
                           V2[:, 2 + t, h * P:(h + 1) * P], t == 0, t == 1, b if t and h == 3 else None)

        def pe_hgrn_scores(pe):
            pe.wait_ge(qk_ready, 1)
            for jc in range(2):
                b = take(pe, ("diag", jc))
                for h in range(HH):
                    mm(ps[:, b, h * P:(h + 1) * P], KE[:, h, jc * P:(jc + 1) * P], Q2[:, h, jc * P:(jc + 1) * P], True, True,
                       b if h == 3 else None)
            for n, (s, d) in enumerate(LEV):
                pe.wait_ge(qk_ready, n + 2)
                for jc in ((d,) if s == P else (0, 1)):
                    b = take(pe, ("lev", n, jc))
                    ic = 1 - jc if s == P else jc
                    for h in range(HH):
                        mm(ps[:, b, h * P:(h + 1) * P], KE[:, h, jc * P:(jc + 1) * P], QE[:, h, ic * P:(ic + 1) * P],
                           True, True, b if h == 3 else None)
                for name, j, jb, _ in beside(n):
                    w = weights(pe, ("in2", jb)).rearrange("p (k n) -> p k n", k=KD)
                    if name == "sv":
                        b = take(pe, (name, j))
                        for k in range(KD):
                            mm(ps[:, b, :], H[:, k, j * P:(j + 1) * P], w[:, k, :], k == 0, k == KD - 1,
                               b if k == KD - 1 else None)
                    else:
                        pe_dense(pe, (name, j), w, (j % 4) * P, H, TX)
                    if j == 1 and name == "sv" or j % 4 == 3:
                        used()
            pe.wait_ge(qk_ready, len(LEV) + 3)
            for g in range(2):
                b = take(pe, ("o2", g))
                for a in range(2):
                    h = 2 * g + a
                    o = ps[:, b, a * TX:(a + 1) * TX]
                    for jc in range(2):
                        mm(o, V2[:, jc, h * P:(h + 1) * P], score_t(jc)[:, h, :], jc == 0, False)
                    mm(o, STATE[:, 0, h, :], QE[:, h, :], False, False)
                    mm(o, STATE[:, 1, h, :], KE[:, h, :], False, True, b if a else None)

        def act_hgrn_scores(c):
            def raw_copies(n):
                for name, j, _, dst in beside(n):
                    b = full_of(c.eng, (name, j))
                    src = ps[:, b, 0:TX] if name != "sv" else ps[:, b, :].rearrange("p (a t) -> p a t", a=2)
                    c.free(S.activation(dst, src, ACT.Copy), (name, j))

            for n in range(len(LEV)):
                c.eng.wait_ge(diff_ready, n + 1)
                c.mark(S.activation(E_[:], E_[:], ACT.Exp), decay_ready, n + 1)
                if n:
                    raw_copies(n - 1)
            raw_copies(len(LEV) - 1)
            for d in range(2):
                c.eng.wait_ge(qk_ready, len(LEV) + 1 + d)
                ins = S.activation(E_[:], BC[d][:, :, 0:TX], ACT.Exp)
                c.mark(ins, decay_ready, len(LEV) + 1 + d)

        def dve_hgrn_scores(c):
            def exponents(n):
                s, d = LEV[n]
                v = BC[d][:, :, 0:TX].rearrange("p h (n w) -> p h n w", w=2 * s)
                e = E_[:].rearrange("p h (n w) -> p h n w", w=2 * s)
                at = s - 1 if d == 0 else s
                mid = v[:, :, :, at:at + 1].broadcast_to([P, HH, TX // (2 * s), s])
                q = slice(s, 2 * s) if d == 0 else slice(0, s)
                k = slice(0, s) if d == 0 else slice(s, 2 * s)
                c.step(V.tensor_tensor(e[:, :, :, q], v[:, :, :, q], mid, ALU.subtract))
                c.mark(V.tensor_tensor(e[:, :, :, k], mid, v[:, :, :, k], ALU.subtract), diff_ready, n + 1)

            c.mark(V.tensor_tensor(KE[:], FG[0][:, :, 0:TX], FG[1][:, :, 0:TX], ALU.add), qk_ready, 1)
            for jc in range(2):
                b = full_of(c.eng, ("diag", jc))
                c.free(V.tensor_copy(score_t(jc)[:, :, jc * P:(jc + 1) * P],
                                     ps[:, b, :].rearrange("p (h i) -> p h i", h=HH)), ("diag", jc))
            exponents(0)
            for n, (s, d) in enumerate(LEV):
                c.eng.wait_ge(decay_ready, n + 1)
                c.step(V.tensor_tensor(QE[:], Q2[:], E_[:], ALU.mult))
                c.mark(V.tensor_tensor(KE[:], FG[d][:, :, 0:TX], E_[:], ALU.mult), qk_ready, n + 2)
                if n + 1 < len(LEV):
                    exponents(n + 1)
                for jc in ((d,) if s == P else (0, 1)):
                    b = full_of(c.eng, ("lev", n, jc))
                    data = ps[:, b, :].rearrange("p (h i) -> p h i", h=HH)
                    if s == P:
                        c.free(V.tensor_copy(score_t(jc)[:, :, (1 - jc) * P:(2 - jc) * P], data), ("lev", n, jc))
                    else:
                        m = 2 * LEVELS.index(s) + d
                        mask = MASK[:, m * P:(m + 1) * P].unsqueeze(1).broadcast_to([P, HH, P])
                        c.free(V.copy_predicated(score_t(jc)[:, :, jc * P:(jc + 1) * P], mask, data), ("lev", n, jc))
            for d in range(2):
                c.eng.wait_ge(decay_ready, len(LEV) + 1 + d)
                c.mark(V.tensor_tensor((QE, KE)[d][:], Q2[:], E_[:], ALU.mult), qk_ready, len(LEV) + 2 + d)
            for g in range(2):
                b = full_of(c.eng, ("o2", g))
                ins = V.tensor_copy(O2[:, 2 * g:2 * g + 2, :], ps[:, b, :].rearrange("p (a t) -> p a t", a=2))
                c.free(ins, ("o2", g))

        G2, U2 = X[:, 0:4, TX:T2], X[:, 4:8, TX:T2]
        SVW = BC[0][:, :, TX:T2]
        YA, GBR = ar(0, KD, TX), ar(2048, KD, TX)
        WS, WST, SGN, SGB = ar(4096, 4, P), ar(4608, 4, P), ar(6144, 512), ar(6656, 512)
        GA_LOW = (BC[1][:, :, TX:T2], ar(5120, 4, TX))

        def gate(n):
            return GA_LOW[n // 4][:, n % 4, :] if n < 8 else GBR[:, n - 8, :]

        def sv(t, g):
            return SVW[:, 2 * t + g // 2, (g % 2) * P:(g % 2 + 1) * P]

        BESIDE = ([("g2", j, 4, G2[:, j, :]) for j in range(4)] + [("u2", j, 5, U2[:, j, :]) for j in range(4)]
                  + [("sv", t, 6, SVW[:, 2 * t:2 * t + 2, :]) for t in range(2)]
                  + [("ga", j, 7 + j // 4, gate(j)) for j in range(8)])

        def beside(n):
            a = 2 * n if n < 4 else n + 4
            return BESIDE[a:a + (2 if n < 4 else 1)]

        HSQ = ar(13312, 2, 512)

        def pe_gates(pe):
            def job_chunks(jb, name, first):
                w = weights(pe, ("in2", jb)).rearrange("p (k n) -> p k n", k=KD)
                for j in range(4):
                    pe_dense(pe, (name, first + j), w, j * P, H, TX)
                used()
            for g in range(2):
                freed(pe, ("o2", g))
            for g in range(2):
                pe_sums(pe, ("hsum", g), 1, lambda k: HSQ[:, g, :], 512,
                        lambda e, k: e.wait_ge(squares_ready.sem, h_sq + g + 1))
            for i in range(2, 4):
                job_chunks(7 + i, "ga", 4 * i)
            b = take(pe, "wst")
            pe.wait_ge(late_loaded, 80)
            for g in range(4):
                m = nc.tensor.transpose(ps[:, b, g * P:(g + 1) * P], WS[:, g, :], ident)
            m.then_inc(bank_full[b], 1)
            freed(pe, "wst")
            for t in range(2):
                pe.wait_ge(sv_ready, t + 1)
                b = take(pe, ("mix", t))
                for g in range(4):
                    mm(ps[:, b, g * P:(g + 1) * P], ft("ones", P, 1), SGB[0:1, g * P:(g + 1) * P], True, False)
                    mm(ps[:, b, g * P:(g + 1) * P], sv(t, g), WST[:, g, :], False, True,
                       b if g == 3 else None)
            pe.wait_ge(o_ready.sem, og_o + 4)
            w = weights(pe, "branch_a").rearrange("p (k n) -> p k n", k=4)
            for n in range(KD):
                pe_dense(pe, ("ya", n), w, n * P, O2, TX, K=4)
            used()
            for t in range(2):
                freed(pe, ("mix", t))
            w = weights(pe, "branch_b").rearrange("p (k n) -> p k n", k=4)
            for n in range(KD):
                pe_dense(pe, ("yb", n), w, n * P, U2, TX, K=4)
            used()
            pe_out(pe, "y2", "out2", lambda k: YA[:, k, :], TX, lambda e: e.wait_ge(y_ready, KD))

        def act_gates(c):
            for g in range(2):
                freed(c.eng, ("o2", g))
                c.mark(S.activation(HSQ[:, g, :], O2[:, 2 * g:2 * g + 2, :].rearrange("p a t -> p (a t)"), ACT.Square),
                         squares_ready, h_sq + g + 1)
            for g in range(2):
                act_rstd(c, ("hsum", g), h_rs + g, P, 512, GR[:, 2 * g:2 * g + 2, :].rearrange("p a t -> p (a t)"))
            c.mark(S.activation(G2, G2, ACT.Silu), gates_ready, 1)
            c.mark(S.activation(SVW, SVW, ACT.Gelu_apprx_tanh), gates_ready, 2)
            c.mark(S.activation(U2, U2, ACT.Gelu_apprx_tanh), gates_ready, 3)
            for i in range(2):
                c.mark(S.activation(GA_LOW[i], GA_LOW[i], ACT.Sigmoid), gates_ready, 4 + i)
            for j in range(8, 16):
                b = full_of(c.eng, ("ga", j))
                c.free(S.activation(gate(j), ps[:, b, 0:TX], ACT.Sigmoid), ("ga", j))
            c.eng.wait_ge(svsum_ready, 1)
            c.step(S.activation(SGS[:, 0:8], SGS[:, 0:8], ACT.Ln, scale=1.0 / P, bias=ft("eps")))
            S.activation(SGS[:, 0:8], SGS[:, 0:8], ACT.Exp, scale=-0.5).then_inc(svr_ready, 1)

        def dve_gates(c):
            for g in range(2):
                c.eng.wait_ge(rstd_ready.sem, h_rs + g + 1)
                for a in range(2):
                    h = 2 * g + a
                    c.step(V.scalar_tensor_tensor(out=O2[:, h, :], in0=O2[:, h, :], scalar=vec("hgrn_norm", h),
                                                  in1=GR[:, h, :], op0=ALU.mult, op1=ALU.mult))
            c.eng.wait_ge(gates_ready, 1)
            for j in range(4):
                c.mark(V.tensor_tensor(O2[:, j, :], O2[:, j, :], G2[:, j, :], ALU.mult), o_ready, og_o + j + 1)
            for t in range(2):
                half = SVW[:, 2 * t:2 * t + 2, :]
                if t == 0:
                    c.eng.wait_ge(gates_ready, 2)
                c.step(V.tensor_tensor(YA[:, 2 * t:2 * t + 2, :], half, half, ALU.mult))
                ins = V.reduce_sum(SGS[:, 4 * t:4 * t + 4],
                                   YA[:, 2 * t:2 * t + 2, :].rearrange("p a (g c) -> p (a g) c", g=2), axis=AX_X)
                (c.mark(ins, svsum_ready, 1) if t else c.step(ins))
            c.eng.wait_ge(late_loaded, 80)
            b = full_of(c.eng, "wst")
            c.free(V.tensor_copy(WST[:], ps[:, b, :].rearrange("p (g t) -> p g t", g=4)), "wst")
            c.eng.wait_ge(svr_ready, 1)
            for t in range(2):
                v4 = SVW[:, 2 * t:2 * t + 2, :].rearrange("p a (g c) -> p a g c", g=2)
                r = SGS[:, 4 * t:4 * t + 4].rearrange("p (a g) -> p a g", a=2).unsqueeze(3).broadcast_to([P, 2, 2, P])
                c.step(V.tensor_tensor(v4, v4, r, ALU.mult))
                half = SVW[:, 2 * t:2 * t + 2, :]
                c.mark(V.tensor_tensor(half, half, SGN.rearrange("p (a t) -> p a t", a=2), ALU.mult), sv_ready, t + 1)
            c.eng.wait_ge(gates_ready, 5)
            for t in range(2):
                b = full_of(c.eng, ("mix", t))
                u = U2[:, :, t * P:(t + 1) * P]
                c.free(V.tensor_tensor(u, u, ps[:, b, :].rearrange("p (g t) -> p g t", g=4), ALU.mult), ("mix", t))
            for n in range(KD):
                b = full_of(c.eng, ("ya", n))
                c.free(V.tensor_tensor(YA[:, n, :], gate(n), ps[:, b, 0:TX], ALU.mult), ("ya", n))
            for n in range(KD):
                b = full_of(c.eng, ("yb", n))
                c.free(V.tensor_tensor(gate(8 + n), gate(8 + n), ps[:, b, 0:TX], ALU.mult), ("yb", n))
                c.mark(V.tensor_tensor(YA[:, n, :], YA[:, n, :], gate(8 + n), ALU.add), y_ready, n + 1)
            for k in range(KD):
                b = full_of(c.eng, ("y2", k))
                c.free(V.scalar_tensor_tensor(out=X[:, k, 0:TX], in0=ps[:, b, 0:TX], scalar=MOD[:, 2, 16 + k, 0:1],
                                              in1=X[:, k, 0:TX], op0=ALU.mult, op1=ALU.add), ("y2", k))

        HTOK = ar(0, 2, D)
        PICK, PICKG = ar(2048, 2, 512), ar(3072, 2, 512)
        XS = ar(4096, KD, NE * CAP)
        SGT = ar(8192, 4, TX)
        YE = ar(9216, 4, D)
        SELR = ar(9216, NE, P)
        AFT = ar(13312, TX)
        EQ = ar(13824, TX)
        BEFORE = ar(14336, 2, TX)
        RW = ar(14848, KD, NE)
        GT, HS, HT = ar(13312, 512), ar(13824, 512), ar(14336, 4, P)
        XSE = ar(14848, 2, KD, CAP)
        AFF, RANK, RST = RTR[:, 0:32], RTR[:, 32:64], RTR[:, 64:72]
        aff3, rank3 = (a.rearrange("p (t e) -> p t e", t=2) for a in (AFF, RANK))

        def pe_route(pe, pre):
            pre.ready(pe)
            for t in range(2):
                b = take(pe, ("rt", t))
                for k in range(KD):
                    mm(ps[:, b, 0:NE], H[:, k, t * P:(t + 1) * P], RW[:, k, :], k == 0, k == KD - 1,
                       b if k == KD - 1 else None)
            for t in range(2):
                for g in range(2):
                    b = take(pe, ("htok", t, g))
                    for k in range(4):
                        m = nc.tensor.transpose(ps[:, b, k * P:(k + 1) * P], H[:, 4 * g + k, t * P:(t + 1) * P], ident)
                    m.then_inc(bank_full[b], 1)
            pe.wait_ge(aff_ready, 1)
            b = take(pe, "aft")
            for t in range(2):
                m = nc.tensor.transpose(ps[0:NE, b, t * P:(t + 1) * P], aff3[:, t, :], ident)
            m.then_inc(bank_full[b], 1)
            freed(pe, "aft")
            for i in range(NE // 2):
                b = take(pe, ("abc", i))
                for a in range(2):
                    mm(ps[:, b, a * TX:(a + 1) * TX], SELR[0:NE, 2 * i + a, :], AFT[0:NE, :], True, True, b if a else None)
            pe.wait_ge(pick_ready, 1)
            for k in range(KD):
                b = take(pe, ("xs", k))
                for t in range(2):
                    mm(ps[:, b, :], HTOK[:, t, k * P:(k + 1) * P], PICK[:, t, :], t == 0, t == 1, b if t else None)
            for g in range(4):
                b = take(pe, ("sgt", g))
                for t in range(2):
                    m = nc.tensor.transpose(ps[:, b, t * P:(t + 1) * P], PICKG[:, t, g * P:(g + 1) * P], ident)
                m.then_inc(bank_full[b], 1)

        def act_route(c):
            for t in range(2):
                for g in range(2):
                    b = full_of(c.eng, ("htok", t, g))
                    c.free(S.activation(HTOK[:, t, g * 512:(g + 1) * 512], ps[:, b, :], ACT.Copy), ("htok", t, g))
            c.eng.wait_ge(rmax_ready, 1)
            for t in range(2):
                b = place[("rt", t)][0]
                c.free(S.activation(aff3[:, t, :], ps[:, b, 0:NE], ACT.Exp, bias=RST[:, 2 + t:3 + t],
                                    accum_out=RST[:, 4 + t:5 + t]), ("rt", t))
            for k in range(KD):
                b = full_of(c.eng, ("xs", k))
                c.free(S.activation(XS[:, k, :], ps[:, b, :], ACT.Copy), ("xs", k))
            for g in range(4):
                b = full_of(c.eng, ("sgt", g))
                c.free(S.activation(SGT[:, g, :], ps[:, b, 0:TX], ACT.Copy), ("sgt", g))

        def dve_route(c):
            for t in range(2):
                b = full_of(c.eng, ("rt", t))
                c.step(V.reduce_max(RST[:, t:t + 1], ps[:, b, 0:NE], axis=AX_X))
            c.mark(V.tensor_scalar(RST[:, 2:4], RST[:, 0:2], -1.0, None, ALU.mult), rmax_ready, 1)
            c.step(V.tensor_copy(SELR[0:NE, :, :], ident[0:NE, 0:NE].unsqueeze(2).broadcast_to([NE, NE, P])))
            for t in range(2):
                freed(c.eng, ("rt", t))
            c.step(V.reciprocal(RST[:, 6:8], RST[:, 4:6]))
            c.mark(V.tensor_tensor(aff3, aff3, RST[:, 6:8].unsqueeze(2).broadcast_to([P, 2, NE]), ALU.mult),
                     aff_ready, 1)
            b = full_of(c.eng, "aft")
            c.free(V.tensor_copy(AFT[0:NE, :], ps[0:NE, b, 0:TX]), "aft")
            for i in range(NE // 2):
                b = full_of(c.eng, ("abc", i))
                for a in range(2):
                    for t in range(2):
                        e = 2 * i + a
                        mine = aff3[:, t, e:e + 1]
                        others = ps[:, b, a * TX:(a + 1) * TX]
                        c.step(V.scalar_tensor_tensor(out=EQ, in0=others, scalar=mine, in1=BEFORE[:, t, :],
                                                      op0=ALU.is_equal, op1=ALU.mult))
                        ins = V.scalar_tensor_tensor(out=EQ, in0=others, scalar=mine, in1=EQ, op0=ALU.is_gt, op1=ALU.add,
                                                     accum_out=rank3[:, t, e:e + 1])
                        (c.free(ins, ("abc", i)) if a and t else c.step(ins))
            for t in range(2):
                p3 = PICK[:, t, :].rearrange("p (e s) -> p e s", e=NE)
                c.step(V.tensor_tensor(p3, ft("slot").unsqueeze(1).broadcast_to([P, NE, CAP]),
                                       rank3[:, t, :].unsqueeze(2).broadcast_to([P, NE, CAP]), ALU.is_equal))
            for t in range(2):
                p3 = PICK[:, t, :].rearrange("p (e s) -> p e s", e=NE)
                g3 = PICKG[:, t, :].rearrange("p (e s) -> p e s", e=NE)
                ins = V.tensor_tensor(g3, p3, aff3[:, t, :].unsqueeze(2).broadcast_to([P, NE, CAP]), ALU.mult)
                (c.mark(ins, pick_ready, 1) if t else c.step(ins))

        w_gate, w_up, w_down = A["expert_w_gate_2"][0], A["expert_w_up_2"][0], A["expert_w_down_2"][0]
        GB, UB, TB, DB = 0, 2, 4, 6

        def sp_experts(sp):
            with sp.Fori(0, NE) as e:
                for j in range(JPE):
                    s = (NJ + j) % SLOTS
                    if j < 8:
                        w = (w_gate, w_up)[j // 4]
                        src = w[bass.ds(e, 1), (j % 4) * 256:(j % 4 + 1) * 256, :].rearrange("a (k p) n -> p (a k) n", p=P)
                        dst = ring[:, s, :].rearrange("p (k n) -> p k n", k=2)
                    else:
                        src = w_down[bass.ds(e, 1), (j - 8) * 512:(j - 7) * 512, :].rearrange("a (k p) n -> p (a k) n", p=P)
                        dst = ring[:, s, :].rearrange("p (k n) -> p k n", k=4)
                    sp.wait_ge(weights_used, e * JPE + (NJ + j - SLOTS + 1))
                    sp.dma_start(dst, src).then_inc(expert_loaded[s], 16)

        def pe_experts(pe):
            for b in range(BANKS):
                pe.wait_ge(bank_free[b], takes[b])
            assert owed[0] == 0
            with pe.Fori(0, NE // 4) as g:
                for q in range(4):
                    par = q % 2
                    pe.wait_ge(xse_ready, g * 4 + (q + 1))
                    for half, bank in ((0, GB), (1, UB)):
                        for i in range(4):
                            j = 4 * half + i
                            s = (NJ + j) % SLOTS
                            pe.wait_ge(expert_loaded[s], (g * 4 + q) * 32 + 16 * (j // SLOTS + 1))
                            w = ring[:, s, :].rearrange("p (k n) -> p k n", k=2)
                            for kk in range(2):
                                k = 2 * i + kk
                                for t in range(4):
                                    m = nc.tensor.matmul(ps[32 * t:32 * t + 32, bank + par, :], lhsT=XSE[:, par, k, :],
                                                         rhs=w[:, kk, t * 512:(t + 1) * 512], start=k == 0, stop=k == 7)
                            m.then_inc(weights_used, 1)
                    pe.wait_ge(hid_done, g * 4 + (q + 2))
                    for i in range(4):
                        m = nc.tensor.transpose(ps[:, TB + par, i * P:(i + 1) * P], HS[:, i * P:(i + 1) * P], ident)
                    m.then_inc(turned, 1)
                    pe.wait_ge(hidt_ready, g * 4 + (q + 1))
                    for i in range(4):
                        j = 8 + i
                        s = (NJ + j) % SLOTS
                        pe.wait_ge(expert_loaded[s], (g * 4 + q) * 32 + 16 * (j // SLOTS + 1))
                        w = ring[:, s, :].rearrange("p (k n) -> p k n", k=4)
                        for cc in range(4):
                            for t in range(4):
                                m = nc.tensor.matmul(ps[32 * t:32 * t + 32, DB + par, 0:TX], lhsT=HT[:, cc, 32 * i:32 * i + 32],
                                                     rhs=w[:, cc, t * TX:(t + 1) * TX], start=i + cc == 0, stop=i + cc == 6)
                        m.then_inc(weights_used, 1)

        def act_experts(c):
            c.step(S.activation(SGS[:, 8:9], ft("eps"), ACT.Silu))
            with c.eng.Fori(0, NE // 4) as g:
                for q in range(4):
                    par = q % 2
                    c.eng.wait_ge(weights_used, (g * 4 + q) * JPE + (NJ + 4))
                    c.eng.wait_ge(hid_done, g * 4 + (q + 1))
                    S.activation(GT, ps[:, GB + par, :], ACT.Silu).then_inc(silu_done, 1)
                    c.eng.wait_ge(turned, g * 4 + (q + 1))
                    S.activation(HT.rearrange("p a b -> p (a b)"), ps[:, TB + par, :], ACT.Copy).then_inc(hidt_ready, 1)

        def dve_experts(c):
            for k in range(KD):
                freed(c.eng, ("xs", k))
            for q in range(2):
                c.mark(V.tensor_copy(XSE[:, q, :, :], XS[:, :, q * CAP:(q + 1) * CAP]), xse_ready, q + 1)
            V.memset(SGS[:, 9:10], 0.0).then_inc(hid_done, 1)
            with c.eng.Fori(0, NE // 4) as g:
                for q in range(4):
                    par = q % 2
                    c.eng.wait_ge(silu_done, g * 4 + (q + 1))
                    c.eng.wait_ge(weights_used, (g * 4 + q) * JPE + (NJ + 8))
                    V.tensor_tensor(HS, GT, ps[:, UB + par, :], ALU.mult).then_inc(hid_done, 1)
                    if q < 2:
                        src = XS[:, :, bass.ds(g * (4 * CAP) + (q + 2) * CAP, CAP)]
                    else:
                        src = XS[:, :, bass.ds((g * (4 * CAP) + (q + 2) * CAP) % (NE * CAP), CAP)]
                    V.tensor_copy(XSE[:, par, :, :], src).then_inc(xse_ready, 1)
                    c.eng.wait_ge(weights_used, (g * 4 + q) * JPE + (NJ + 12))
                    for t in range(4):
                        dst = YE[32 * q:32 * q + 32, bass.ds(g, 1), t * TX:(t + 1) * TX].rearrange("p a n -> p (a n)")
                        ins = V.tensor_copy(dst, ps[32 * t:32 * t + 32, DB + par, 0:TX])
                    ins.then_inc(ye_ready, 1)

        OUT = ar(0, 2, D)

        def pe_combine(pe):
            pe.wait_ge(ye_ready, NE)
            for k in range(KD):
                b = take(pe, ("comb", k))
                for g in range(4):
                    mm(ps[:, b, 0:TX], YE[:, g, k * P:(k + 1) * P], SGT[:, g, :], g == 0, g == 3, b if g == 3 else None)

        def dve_combine(c):
            for k in range(KD):
                b = full_of(c.eng, ("comb", k))
                c.free(V.scalar_tensor_tensor(out=X[:, k, 0:TX], in0=ps[:, b, 0:TX], scalar=MOD[:, 2, 40 + k, 0:1],
                                              in1=X[:, k, 0:TX], op0=ALU.mult, op1=ALU.add), ("comb", k))

        def pe_final(pe):
            pe_sums(pe, "sum_final", KD, lambda k: H[:, k, 0:TX], TX,
                    lambda e, k: e.wait_ge(squares_ready.sem, fin_sq + k + 1))
            for g in range(2):
                for t in range(2):
                    b = take(pe, ("out", t, g))
                    pe.wait_ge(fin_ready, 4 * g + 4)
                    for k in range(4):
                        m = nc.tensor.transpose(ps[:, b, k * P:(k + 1) * P], X[:, 4 * g + k, t * P:(t + 1) * P], ident)
                    m.then_inc(bank_full[b], 1)

        def act_final(c):
            act_squares(c, fin_sq, KD, lambda k: X[:, k, 0:TX], lambda k: H[:, k, 0:TX],
                        lambda e, k: freed(e, ("comb", k)))
            act_rstd(c, "sum_final", fin_rs, D, TX, RS[:, 0:TX])

        def dve_final(c):
            c.eng.wait_ge(rstd_ready.sem, fin_rs + 1)
            for k in range(KD):
                c.mark(V.scalar_tensor_tensor(out=X[:, k, 0:TX], in0=X[:, k, 0:TX], scalar=vec("final", k),
                                                in1=RS[:, 0:TX], op0=ALU.mult, op1=ALU.mult), fin_ready, k + 1)
            for g in range(2):
                for t in range(2):
                    b = full_of(c.eng, ("out", t, g))
                    c.free(V.tensor_copy(OUT[:, t, g * 512:(g + 1) * 512], ps[:, b, :]), ("out", t, g))

        pre0a = Pre("pre0a", 0, 0, 2)
        sub_sq, sub_rs, sub_o = squares_ready.plan(4), rstd_ready.plan(4), o_ready.plan(4)
        attn0 = Attention(ab_units, pe_ada_beside, dve_ada_beside)
        y_at = [ar(0, KD, T2), ar(4096, KD, T2)]
        post0a = Post("y0", 0, 0, 2, lambda k: y_at[0][:, k, :], lambda k: y_at[1][:, k, :])
        pre0f = Pre("pre0f", 0, 1, 2)
        yf = ar(11264, KD, T2)
        post0f = Post(("ffn", 0), 0, 1, 2, lambda k: yf[:, k, :], lambda k: H[:, k, :])
        pre1a = Pre("pre1a", 1, 0, 2)
        lat_rs, krope, qrope = rstd_ready.plan(2), roped.plan(1), roped.plan(8)
        attn1 = Attention(mla_units)
        y1 = [ar(8192, KD, TX), ar(10240, KD, TX)]
        post1a = Post("y1", 1, 0, 1, lambda k: y1[0][:, k, :], lambda k: y1[1][:, k, :])
        pre1f = Pre("pre1f", 1, 1, 1)
        yg = ar(5632, KD, TX)
        post1f = Post(("ffn", 1), 1, 1, 1, lambda k: yg[:, k, :], lambda k: H[:, k, 0:TX])
        pre2a = Pre("pre2a", 2, 0, 2)
        h_sq, h_rs, og_o = squares_ready.plan(2), rstd_ready.plan(2), o_ready.plan(4)
        pre2f = Pre("pre2f", 2, 1, 1)
        fin_sq, fin_rs = squares_ready.plan(KD), rstd_ready.plan(1)

        CTX2 = ar(8192, 2, D)
        XIN = ar(0, 4, D)
        VROW = ar(4096, 3, P)
        LV = ar(4480, 4, 64)
        MASKF = ar(4736, MASK_W)

        block = es.enter_context(nc.Block())

        @block.tensor
        def _(pe):
            pe_vectors(pe)
            pe_load(pe, "x0", XIN, 4, lambda e: e.wait_ge(x_loaded, 32))
            pe_adaln0(pe)
            pre0a.pe(pe)
            pe_ab_in(pe, pre0a)
            pe.wait_ge(roped.sem, rope_base + len(ROPED))
            for t in range(4):
                freed(pe, ("v", 4, t))
            attn0.pe(pe)
            for i in range(len(ab_units), len(ab_units) + 3):
                pe_ada_beside(pe, i)
            pe_subln(pe)
            pe_out(pe, "y0", "ab_out", lambda k: H[:, k, :], T2, lambda e: e.wait_ge(o_ready.sem, sub_o + 4))
            post0a.pe(pe)
            pre0f.pe(pe)
            pe_ffn(pe, 0, T2, pre0f)
            post0f.pe(pe)
            pre1a.pe(pe)
            pe_mla_in(pe, pre1a)
            pe.wait_ge(roped.sem, qrope + 8)
            for h in range(CH):
                freed(pe, ("km", h))
            for t in range(4):
                for g in range(2):
                    freed(pe, ("vm", t, g))
            attn1.pe(pe)
            for qc in range(2):
                freed(pe, ("o", ("m", CH - 1, qc)))
            pe_out(pe, "y1", "mla_out", lambda k: KM[:, 2 * k, 0:TX], TX, lambda e: None)
            post1a.pe(pe)
            pre1f.pe(pe)
            pe_ffn(pe, 1, TX, pre1f)
            post1f.pe(pe)
            pe_load(pe, "ctx2", CTX2, 2, lambda e: e.wait_ge(ctx_loaded, 16))
            pre2a.pe(pe)
            pe_hgrn_in(pe, pre2a)
            pe_hgrn_state(pe)
            pe_hgrn_scores(pe)
            pe_gates(pe)
            pre2f.pe(pe)
            pe_route(pe, pre2f)
            if last > 1:
                pe_experts(pe)
                pe_combine(pe)
                pe_final(pe)

        @block.sync
        def _(sp):
            sp.wait_ge(small_loaded, SMALL)
            for j, dmas in enumerate(jobs):
                s = j % SLOTS
                if j >= SLOTS:
                    sp.wait_ge(weights_used, j - SLOTS + 1)
                for dst, src in dmas:
                    sp.dma_start(dst(s), src).then_inc(slot_loaded[s], 16)
            if last > 1:
                sp_experts(sp)
                for t in range(2):
                    for g in range(2):
                        freed(sp, ("out", t, g))
                sp.dma_start(out[0].rearrange("(t p) n -> p t n", p=P), OUT[:]).then_inc(out_written, 16)
                sp.wait_ge(out_written, 16)

        @block.gpsimd
        def _(pool):
            pool.dma_start(LV.rearrange("p a b -> p (a b)"), A["diff_lambda"].rearrange("l a b -> l (a b)")
                           .broadcast_to([P, 256])).then_inc(side_loaded, 16)
            pool.dma_start(SINK[:], A["ab_sink"][0:1, :].broadcast_to([P, AH])).then_inc(side_loaded, 16)
            pool.dma_start(MASKF, tab_m).then_inc(side_loaded, 16)
            for i, w in enumerate(("x", "ctx")):
                pool.dma_start(XIN[:, 2 * i:2 * i + 2, :], A[w][0].rearrange("(t p) n -> p t n", p=P)
                               ).then_inc(x_loaded, 16)
            pool.wait_ge(x_ready.sem, post1a.x + KD)
            pool.dma_start(CTX2, A["ctx_2"][0].rearrange("(t p) n -> p t n", p=P)).then_inc(ctx_loaded, 16)
            for g in range(2):
                freed(pool, ("o2", g))
            pool.dma_start(WS, A["sgu_w_2"][0].rearrange("g t s -> t g s")).then_inc(late_loaded, 16)
            pool.dma_start(SGN, A["sgu_norm_w_2"][0:1, :].broadcast_to([P, 512])).then_inc(late_loaded, 16)
            pool.dma_start(BEFORE, tab_f[:, FT_W:TAB_W].rearrange("p (t k) -> p t k", t=2)).then_inc(late_loaded, 16)
            pool.dma_start(RW, A["router_w_2"][0].rearrange("(k p) e -> p k e", p=P)).then_inc(late_loaded, 16)
            pool.dma_start(SGB[0:1, :], A["sgu_b_2"].rearrange("l g t -> l (g t)")).then_inc(late_loaded, 16)

        @block.scalar
        def _(act):
            c = Chain(act, act_step)
            act.dma_start(VROW, vrows).then_inc(small_loaded, 16)
            act.dma_start(FTAB[:], tab_f[:, 0:FT_W]).then_inc(small_loaded, 16)
            act.wait_ge(small_loaded, SMALL)
            act_cond(c)
            pre0a.act(c, lambda e, k: freed(e, ("x0", k)))
            act_ab_in(c)
            attn0.act(c)
            act_subln(c)
            post0a.act(c)
            pre0f.act(c, lambda e, k: e.wait_ge(x_ready.sem, post0a.x + k + 1))
            act_ffn(c, 0, T2)
            post0f.act(c)
            pre1a.act(c, lambda e, k: e.wait_ge(x_ready.sem, post0f.x + k + 1))
            act_mla_in(c)
            attn1.act(c)
            post1a.act(c)
            pre1f.act(c, lambda e, k: e.wait_ge(x_ready.sem, post1a.x + k + 1))
            act_ffn(c, 1, TX)
            post1f.act(c)
            pre2a.act(c, lambda e, k: freed(e, ("ctx2", k)))
            act_hgrn_in(c)
            act_hgrn_scores(c)
            act_gates(c)
            pre2f.act(c, lambda e, k: freed(e, ("y2", k)))
            act_route(c)
            if last > 1:
                act_experts(c)
                act_final(c)

        @block.vector
        def _(dve):
            c = Chain(dve, dve_step)
            dve.wait_ge(small_loaded, SMALL)
            dve_vectors(c)
            dve_load(c, "x0", 0, T2)
            dve_small(c)
            dve_adaln0(c)
            pre0a.dve(c)
            dve_ab_in(c)
            attn0.dve(c)
            for i in range(len(ab_units), len(ab_units) + 3):
                dve_ada_beside(c, i)
            for l in (1, 2):
                dve_mods(c, l)
            dve_subln(c)
            post0a.dve(c)
            pre0f.dve(c)
            dve_ffn(c, 0, T2)
            post0f.dve(c)
            pre1a.dve(c)
            dve_mla_in(c)
            attn1.dve(c)
            post1a.dve(c)
            pre1f.dve(c)
            dve_ffn(c, 1, TX)
            post1f.dve(c)
            dve_load(c, "ctx2", TX, TX)
            pre2a.dve(c)
            dve_hgrn_in(c)
            dve_hgrn_scores(c)
            dve_gates(c)
            pre2f.dve(c)
            dve_route(c)
            if last > 1:
                dve_experts(c)
                dve_combine(c)
                dve_final(c)

_INS = ['x', 'ctx', 'ada_w', 'ffn_w13', 'ffn_w2', 'ab_w_in', 'ab_w_out', 'ab_sink',
        'diff_lambda', 'mla_w_in', 'mla_wq_b', 'mla_wkv_b',
        'mla_w_out', 'ctx_2', 'ada_w_2', 'w_in_2',
        'sgu_norm_w_2', 'sgu_w_2', 'sgu_b_2', 'w_branch_a_2', 'w_branch_b_2',
        'w_out_2', 'router_w_2', 'expert_w_gate_2', 'expert_w_up_2', 'expert_w_down_2']

def kernel(**inputs):
    import numpy as _np
    import concourse.bacc as _bacc
    from concourse import mybir as _mybir
    from concourse.bass_utils import run_bass_kernel_spmd as _run

    nc = _bacc.Bacc("TRN2", target_bir_lowering=False, num_devices=1)
    arrays, args = {}, {}
    tab_f, tab_m = tables()
    extra = {"tab_f": tab_f, "tab_m": tab_m, "vrows": vector_rows(inputs)}
    for name in _INS + list(extra):
        a = extra.get(name)
        if a is None:
            a = _np.ascontiguousarray(inputs[name])
        arrays[f"in_{name}"] = a
        args[name] = nc.dram_tensor(f"in_{name}", a.shape, _mybir.dt.from_np(a.dtype), kind="ExternalInput").ap()
    out = nc.dram_tensor("out_0", (1, TX, D), F32, kind="ExternalOutput").ap()
    build(nc, args, args["tab_f"], args["tab_m"], args["vrows"], out)
    r = _run(nc, [arrays], core_ids=[0])
    return r.results[0]["out_0"]
```
